# Optimizing a Trainium2 kernel written in Bass

```python
import jax, jax.numpy as jnp
from jax import lax
import numpy as np

D_MODEL = 1024
BATCH = 1
SEQ = 256
DEPTH = 1

N_MIXERS = 4
RMS_EPS = 1e-6
N_MOD = 6

SB_HEADS = 16
SB_HEAD_DIM = D_MODEL // SB_HEADS
SB_QBLOCK = 128

GLA_HEADS = 4
GLA_DK = D_MODEL // (2 * GLA_HEADS)
GLA_DV = D_MODEL // GLA_HEADS
GLA_GATE_RANK = 16
GLA_GATE_TAU = 16.0
GLA_CHUNK = 64
GLA_IN = 2 * GLA_HEADS * GLA_DK + 2 * GLA_HEADS * GLA_DV + GLA_GATE_RANK

CONV_WIDTH = 3

DIL_PATTERNS = ((128, 1), (512, 4), (2048, 16))
DIL_GROUPS = len(DIL_PATTERNS)
DIL_HEADS = 8
DIL_HEAD_DIM = 64
DIL_QBLOCK = 128

MOE_GROUPS = 4
MOE_PER_GROUP = 8
MOE_EXPERTS = MOE_GROUPS * MOE_PER_GROUP
MOE_TOPK = 2
MOE_D_FF = D_MODEL // 2
MOE_BLOCK = 128

N_SB = (DEPTH + 3) // N_MIXERS
N_GLA = (DEPTH + 2) // N_MIXERS
N_CONV = (DEPTH + 1) // N_MIXERS
N_DIL = DEPTH // N_MIXERS


def rms_norm(x, g):
    x32 = x.astype(jnp.float32)
    y = x32 * lax.rsqrt(jnp.mean(x32 * x32, axis=-1, keepdims=True) + RMS_EPS)
    return (y * g.astype(jnp.float32)).astype(x.dtype)

def stick_breaking_attention(q, k, v):
    B, H, S, d = q.shape
    nb = S // SB_QBLOCK
    scale = d ** -0.5
    kpos = jnp.arange(S)
    qb = jnp.moveaxis(q.reshape(B, H, nb, SB_QBLOCK, d), 2, 0)

    def one_block(args):
        q_blk, blk = args
        qpos = blk * SB_QBLOCK + jnp.arange(SB_QBLOCK)
        z = jnp.einsum('bhqd,bhkd->bhqk', q_blk, k, preferred_element_type=jnp.float32) * scale
        causal = kpos[None, :] < qpos[:, None]
        log_keep = jnp.where(causal, jax.nn.log_sigmoid(-z), 0.0)
        suffix = lax.cumsum(log_keep, axis=3, reverse=True) - log_keep
        a = jnp.where(causal, jnp.exp(jax.nn.log_sigmoid(z) + suffix), 0.0)
        return jnp.einsum('bhqk,bhkd->bhqd', a.astype(v.dtype), v)

    out = lax.map(one_block, (qb, jnp.arange(nb)))
    return jnp.moveaxis(out, 0, 2).reshape(B, H, S, d)

def sb_mixer(h, w_in, w_out):
    B, S, _ = h.shape
    qkv = (h @ w_in).reshape(B, S, 3, SB_HEADS, SB_HEAD_DIM)
    qkv = jnp.transpose(qkv, (2, 0, 3, 1, 4))
    o = stick_breaking_attention(qkv[0], qkv[1], qkv[2])
    return jnp.transpose(o, (0, 2, 1, 3)).reshape(B, S, SB_HEADS * SB_HEAD_DIM) @ w_out

def gla_chunked(q, k, v, log_a):
    B, H, S, dk = q.shape
    dv = v.shape[-1]
    C = GLA_CHUNK
    nc = S // C
    f32 = jnp.float32

    def chunks(a):
        return a.astype(f32).reshape(B, H, nc, C, a.shape[-1])

    q, k, v, g = chunks(q), chunks(k), chunks(v), chunks(log_a)
    b = jnp.cumsum(g, axis=3)
    b_last = b[:, :, :, -1:, :]
    q_in = q * jnp.exp(b)
    k_in = k * jnp.exp(-b)
    k_state = k * jnp.exp(b_last - b)
    causal = jnp.tril(jnp.ones((C, C), dtype=bool))
    scores = jnp.where(causal, jnp.einsum('bhnid,bhnjd->bhnij', q_in, k_in), 0.0)
    o_intra = jnp.einsum('bhnij,bhnjv->bhniv', scores, v)

    def step(state, inp):
        q_n, k_n, v_n, decay_n = inp
        o_n = jnp.einsum('bhid,bhdv->bhiv', q_n, state)
        state = decay_n[..., None] * state + jnp.einsum('bhjd,bhjv->bhdv', k_n, v_n)
        return state, o_n

    xs = (jnp.moveaxis(q_in, 2, 0), jnp.moveaxis(k_state, 2, 0), jnp.moveaxis(v, 2, 0),
          jnp.moveaxis(jnp.exp(b_last[:, :, :, 0, :]), 2, 0))
    _, o_inter = lax.scan(step, jnp.zeros((B, H, dk, dv), f32), xs)
    o = o_intra + jnp.moveaxis(o_inter, 0, 2)
    return o.reshape(B, H, S, dv)

def gla_mixer(h, w_in, w_gate_up, b_gate, norm_g, w_out):
    B, S, _ = h.shape
    dqk = GLA_HEADS * GLA_DK
    dv = GLA_HEADS * GLA_DV
    proj = h @ w_in
    q, k, v, r, g_down = jnp.split(proj, [dqk, 2 * dqk, 2 * dqk + dv, 2 * dqk + 2 * dv], axis=-1)
    log_a = jax.nn.log_sigmoid((g_down @ w_gate_up + b_gate).astype(jnp.float32)) / GLA_GATE_TAU

    def heads(a, d):
        return jnp.transpose(a.reshape(B, S, GLA_HEADS, d), (0, 2, 1, 3))

    o = gla_chunked(heads(q, GLA_DK) * GLA_DK ** -0.5, heads(k, GLA_DK),
                    heads(v, GLA_DV), heads(log_a, GLA_DK))
    o = rms_norm(o, norm_g)
    o = jnp.transpose(o, (0, 2, 1, 3)).reshape(B, S, dv).astype(h.dtype) * jax.nn.silu(r)
    return o @ w_out

def conv_mixer(h, w_in, conv_w, conv_b, w_out):
    S = h.shape[1]
    gate_b, gate_c, u = jnp.split(h @ w_in, 3, axis=-1)
    u = gate_c * u
    u_pad = jnp.pad(u, ((0, 0), (CONV_WIDTH - 1, 0), (0, 0)))
    y = sum(conv_w[j] * u_pad[:, j:j + S] for j in range(CONV_WIDTH)) + conv_b
    return (gate_b * y) @ w_out

def dilated_window_attention(q, k, v, window, dilation):
    B, H, S, d = q.shape
    Q = DIL_QBLOCK
    steps = window // dilation
    span = dilation * Q
    Sp = -(-S // span) * span
    L = Sp // dilation
    nb = L // Q

    def strided(a):
        a = jnp.pad(a, ((0, 0), (0, 0), (0, Sp - S), (0, 0)))
        a = jnp.transpose(a.reshape(B, H, L, dilation, d), (0, 1, 3, 2, 4))
        return a.reshape(B, H, dilation, nb, Q, d)

    def with_prev(a):
        prev = jnp.concatenate([jnp.zeros_like(a[:, :, :, :1]), a[:, :, :, :-1]], axis=3)
        return jnp.concatenate([prev, a], axis=4)

    qb = strided(q)
    kc, vc = with_prev(strided(k)), with_prev(strided(v))
    z = jnp.einsum('bhrnqd,bhrnkd->bhrnqk', qb, kc, preferred_element_type=jnp.float32) * d ** -0.5
    qi = jnp.arange(Q)[:, None]
    kj = jnp.arange(2 * Q)[None, :]
    dist = qi + Q - kj
    in_window = (dist >= 0) & (dist <= steps)
    before_start = (jnp.arange(nb)[:, None, None] == 0) & (kj < Q)[None]
    valid = in_window[None] & ~before_start
    z = jnp.where(valid, z, -jnp.inf)
    m = jnp.max(z, axis=-1, keepdims=True)
    lse = m + jnp.log(jnp.sum(jnp.exp(z - m), axis=-1, keepdims=True))
    p = jnp.exp(z - lse)
    o = jnp.einsum('bhrnqk,bhrnkd->bhrnqd', p.astype(vc.dtype), vc)

    def unstride(a):
        e = a.shape[-1]
        a = jnp.moveaxis(a.reshape(B, H, dilation, L, e), 2, 3).reshape(B, H, Sp, e)
        return a[:, :, :S]

    return unstride(o), unstride(lse)[..., 0]

def dil_mixer(h, w_in, w_out):
    B, S, _ = h.shape
    proj = (h @ w_in).reshape(B, S, DIL_GROUPS, 3, DIL_HEADS, DIL_HEAD_DIM)
    proj = jnp.transpose(proj, (2, 3, 0, 4, 1, 5))
    outs, lses = [], []
    for g, (window, dilation) in enumerate(DIL_PATTERNS):
        o_g, lse_g = dilated_window_attention(proj[g, 0], proj[g, 1], proj[g, 2], window, dilation)
        outs.append(o_g)
        lses.append(lse_g)
    o = jnp.stack(outs)
    w = jax.nn.softmax(jnp.stack(lses), axis=0)
    o = jnp.einsum('gbhs,gbhsd->bshd', w.astype(o.dtype), o).reshape(B, S, DIL_HEADS * DIL_HEAD_DIM)
    return o @ w_out

def hier_moe(h, w_grp, b_grp, w_exp, b_exp, w_gate, w_up, w_down):
    T, D = h.shape
    f32 = jnp.float32
    grp_logits = (h @ w_grp + b_grp).astype(f32)
    grp = jnp.argmax(grp_logits, axis=-1)
    p_grp = jnp.take_along_axis(jax.nn.softmax(grp_logits, axis=-1), grp[:, None], axis=-1)
    exp_logits = (h @ w_exp + b_exp).astype(f32).reshape(T, MOE_GROUPS, MOE_PER_GROUP)
    in_grp = jnp.take_along_axis(exp_logits, grp[:, None, None], axis=1)[:, 0]
    p_in, top_i = lax.top_k(jax.nn.softmax(in_grp, axis=-1), MOE_TOPK)
    gate = p_grp * p_in / jnp.sum(p_in, axis=-1, keepdims=True)
    expert = grp[:, None] * MOE_PER_GROUP + top_i

    A = T * MOE_TOPK
    flat_e = expert.reshape(A)
    order = jnp.argsort(flat_e)
    sorted_e = flat_e[order]
    sorted_tok = order // MOE_TOPK
    sorted_w = gate.reshape(A)[order]
    counts = jnp.bincount(flat_e, length=MOE_EXPERTS)
    padded = (counts + MOE_BLOCK - 1) // MOE_BLOCK * MOE_BLOCK
    pad_end = jnp.cumsum(padded)
    pad_start = pad_end - padded
    start = jnp.cumsum(counts) - counts
    dest = pad_start[sorted_e] + jnp.arange(A) - start[sorted_e]
    P = (-(-A // MOE_BLOCK) + MOE_EXPERTS) * MOE_BLOCK
    NB = P // MOE_BLOCK
    slot_tok = jnp.full((P,), T, dtype=jnp.int32).at[dest].set(sorted_tok.astype(jnp.int32))
    slot_w = jnp.zeros((P,), f32).at[dest].set(sorted_w)
    blk_e = jnp.minimum(jnp.searchsorted(pad_end, jnp.arange(NB) * MOE_BLOCK, side='right'),
                        MOE_EXPERTS - 1)
    h_pad = jnp.concatenate([h, jnp.zeros((1, D), h.dtype)], axis=0)
    xb = h_pad[slot_tok].reshape(NB, MOE_BLOCK, D)

    def expert_block(args):
        x_blk, e = args
        return (jax.nn.silu(x_blk @ w_gate[e]) * (x_blk @ w_up[e])) @ w_down[e]

    yb = lax.map(expert_block, (xb, blk_e)).reshape(P, D)
    y = jax.ops.segment_sum(yb.astype(f32) * slot_w[:, None], slot_tok, num_segments=T + 1)[:T]
    return y.astype(h.dtype)

def first_inputs(seed: int = 0) -> dict:
    key = jax.random.key(seed)
    keys = jax.random.split(key, 26)
    D = D_MODEL

    def nrm(i, shape, scale):
        return jax.random.normal(keys[i], shape, jnp.float32) * scale

    sb_w = SB_HEADS * SB_HEAD_DIM
    gla_dqk = GLA_HEADS * GLA_DK
    gla_dv = GLA_HEADS * GLA_DV
    dil_w = DIL_HEADS * DIL_HEAD_DIM
    return {
        "x": nrm(0, (BATCH, SEQ, D), 1.0),
        "c": nrm(1, (BATCH, D), 1.0),
        "ada_w": nrm(2, (DEPTH, D, N_MOD * D), 0.5 * D ** -0.5),
        "ada_b": nrm(3, (DEPTH, N_MOD * D), 0.01),
        "norm_g": 1.0 + nrm(4, (DEPTH, 2, D), 0.02),
        "final_g": 1.0 + nrm(5, (D,), 0.02),
        "sb_w_in": nrm(6, (N_SB, D, 3 * sb_w), D ** -0.5),
        "sb_w_out": nrm(7, (N_SB, sb_w, D), sb_w ** -0.5),
        "gla_w_in": nrm(8, (N_GLA, D, GLA_IN), D ** -0.5),
        "gla_w_gate_up": nrm(9, (N_GLA, GLA_GATE_RANK, gla_dqk), GLA_GATE_RANK ** -0.5),
        "gla_b_gate": nrm(10, (N_GLA, gla_dqk), 0.01),
        "gla_norm_g": 1.0 + nrm(11, (N_GLA, GLA_DV), 0.02),
        "gla_w_out": nrm(12, (N_GLA, gla_dv, D), gla_dv ** -0.5),
        "conv_w_in": nrm(13, (N_CONV, D, 3 * D), D ** -0.5),
        "conv_w": nrm(14, (N_CONV, CONV_WIDTH, D), CONV_WIDTH ** -0.5),
        "conv_b": nrm(15, (N_CONV, D), 0.01),
        "conv_w_out": nrm(16, (N_CONV, D, D), D ** -0.5),
        "dil_w_in": nrm(17, (N_DIL, D, DIL_GROUPS * 3 * dil_w), D ** -0.5),
        "dil_w_out": nrm(18, (N_DIL, dil_w, D), dil_w ** -0.5),
        "moe_w_grp": nrm(19, (DEPTH, D, MOE_GROUPS), D ** -0.5),
        "moe_b_grp": nrm(20, (DEPTH, MOE_GROUPS), 0.01),
        "moe_w_exp": nrm(21, (DEPTH, D, MOE_EXPERTS), D ** -0.5),
        "moe_b_exp": nrm(22, (DEPTH, MOE_EXPERTS), 0.01),
        "moe_w_gate": nrm(23, (DEPTH, MOE_EXPERTS, D, MOE_D_FF), D ** -0.5),
        "moe_w_up": nrm(24, (DEPTH, MOE_EXPERTS, D, MOE_D_FF), D ** -0.5),
        "moe_w_down": nrm(25, (DEPTH, MOE_EXPERTS, MOE_D_FF, D), MOE_D_FF ** -0.5),
    }

def first_block(x, c, ada_w, ada_b, norm_g, final_g, sb_w_in, sb_w_out, gla_w_in, gla_w_gate_up,
              gla_b_gate, gla_norm_g, gla_w_out, conv_w_in, conv_w, conv_b, conv_w_out,
              dil_w_in, dil_w_out, moe_w_grp, moe_b_grp, moe_w_exp, moe_b_exp, moe_w_gate,
              moe_w_up, moe_w_down):
    B, S, D = x.shape
    cond = jax.nn.silu(c)
    for i in range(DEPTH):
        mod = cond @ ada_w[i] + ada_b[i]
        sh1, sc1, g1, sh2, sc2, g2 = jnp.split(mod[:, None, :], N_MOD, axis=-1)

        h = rms_norm(x, norm_g[i, 0]) * (1.0 + sc1) + sh1
        kind, j = i % N_MIXERS, i // N_MIXERS
        if kind == 0:
            y = sb_mixer(h, sb_w_in[j], sb_w_out[j])
        elif kind == 1:
            y = gla_mixer(h, gla_w_in[j], gla_w_gate_up[j], gla_b_gate[j], gla_norm_g[j], gla_w_out[j])
        elif kind == 2:
            y = conv_mixer(h, conv_w_in[j], conv_w[j], conv_b[j], conv_w_out[j])
        else:
            y = dil_mixer(h, dil_w_in[j], dil_w_out[j])
        x = (x + g1 * y).astype(x.dtype)

        h = rms_norm(x, norm_g[i, 1]) * (1.0 + sc2) + sh2
        y = hier_moe(h.reshape(B * S, D), moe_w_grp[i], moe_b_grp[i], moe_w_exp[i], moe_b_exp[i],
                     moe_w_gate[i], moe_w_up[i], moe_w_down[i]).reshape(B, S, D)
        x = (x + g2 * y).astype(x.dtype)
    return rms_norm(x, final_g)


CHUNK = 64
M_HEADS = 4
M_HEAD_DIM = D_MODEL // M_HEADS
M_WIDTH = M_HEADS * M_HEAD_DIM
CONV_K = 4
SGU_BLOCK = 128
SGU_GROUPS = 4
SGU_WIDTH = D_MODEL
SGU_GROUP_DIM = SGU_WIDTH // SGU_GROUPS
D_FF = 2816
PROJ_SIZES = (M_WIDTH, M_WIDTH, M_WIDTH, M_WIDTH, M_HEADS, M_HEADS, 2 * SGU_WIDTH, D_MODEL, D_MODEL)
N_PROJ = 4 * M_WIDTH + 2 * M_HEADS + 2 * SGU_WIDTH + 2 * D_MODEL
LN_EPS = 1e-5


def rmsnorm(x, g):
    x32 = x.astype(jnp.float32)
    y = x32 * lax.rsqrt(jnp.mean(x32 * x32, axis=-1, keepdims=True) + RMS_EPS)
    return (y * g.astype(jnp.float32)).astype(x.dtype)

def layernorm32(x, eps):
    x32 = x.astype(jnp.float32)
    xc = x32 - jnp.mean(x32, axis=-1, keepdims=True)
    return xc * lax.rsqrt(jnp.mean(xc * xc, axis=-1, keepdims=True) + eps)

def swiglu(x, w_in, w_out):
    gate, up = jnp.split(x @ w_in, 2, axis=-1)
    return (jax.nn.silu(gate) * up) @ w_out

def causal_depthwise_conv(x, w, b):
    y = lax.conv_general_dilated(
        x, w[:, None, :].astype(x.dtype), window_strides=(1,),
        padding=[(CONV_K - 1, 0)], dimension_numbers=('NWC', 'WIO', 'NWC'),
        feature_group_count=x.shape[-1])
    return y + b.astype(x.dtype)

def mlstm_chunkwise(q, k, v, log_i, log_f):
    bsz, nh, seqlen, dh = q.shape
    nc = seqlen // CHUNK

    def to_chunks(t):
        return jnp.moveaxis(t.reshape(bsz, nh, nc, CHUNK, *t.shape[3:]), 2, 0)

    causal = jnp.tril(jnp.ones((CHUNK, CHUNK), dtype=bool))

    def step(carry, xs):
        c_state, n_state, m_state = carry
        qc, kc, vc, lic, lfc = xs
        b = jnp.cumsum(lfc, axis=-1)
        a_inter = b + m_state[..., None]
        d = jnp.where(causal, b[..., :, None] - b[..., None, :] + lic[..., None, :], -jnp.inf)
        m_t = jnp.maximum(a_inter, jnp.max(d, axis=-1))
        w_inter = jnp.exp(a_inter - m_t)
        scores = jnp.einsum('bhtd,bhsd->bhts', qc, kc) * jnp.exp(d - m_t[..., None])
        num = (w_inter[..., None] * jnp.einsum('bhed,bhtd->bhte', c_state, qc)
               + jnp.einsum('bhts,bhse->bhte', scores, vc))
        den = w_inter * jnp.einsum('bhd,bhtd->bht', n_state, qc) + jnp.sum(scores, axis=-1)
        h = num / jnp.maximum(jnp.abs(den), jnp.exp(-m_t))[..., None]
        b_last = b[..., -1]
        g = b_last[..., None] - b + lic
        m_new = jnp.maximum(b_last + m_state, jnp.max(g, axis=-1))
        decay = jnp.exp(b_last + m_state - m_new)
        wk = jnp.exp(g - m_new[..., None])
        c_new = decay[..., None, None] * c_state + jnp.einsum('bhs,bhse,bhsd->bhed', wk, vc, kc)
        n_new = decay[..., None] * n_state + jnp.einsum('bhs,bhsd->bhd', wk, kc)
        return (c_new, n_new, m_new), h

    init = (jnp.zeros((bsz, nh, dh, dh), jnp.float32),
            jnp.zeros((bsz, nh, dh), jnp.float32),
            jnp.zeros((bsz, nh), jnp.float32))
    xs = (to_chunks(q), to_chunks(k), to_chunks(v), to_chunks(log_i), to_chunks(log_f))
    _, hs = lax.scan(step, init, xs)
    return jnp.moveaxis(hs, 0, 2).reshape(bsz, nh, seqlen, dh)

def mlstm_branch(q_pre, k_pre, v_pre, o_pre, i_pre, f_pre, conv_w, conv_b, b_i, b_f, head_g):
    bsz, seqlen, _ = q_pre.shape
    qk = jax.nn.silu(causal_depthwise_conv(jnp.concatenate([q_pre, k_pre], axis=-1), conv_w, conv_b))
    q, k = jnp.split(qk, 2, axis=-1)

    def heads(t):
        return t.reshape(bsz, seqlen, M_HEADS, M_HEAD_DIM).transpose(0, 2, 1, 3).astype(jnp.float32)

    log_i = (i_pre + b_i).astype(jnp.float32).transpose(0, 2, 1)
    log_f = jax.nn.log_sigmoid((f_pre + b_f).astype(jnp.float32)).transpose(0, 2, 1)
    h = mlstm_chunkwise(heads(q), heads(k) * (M_HEAD_DIM ** -0.5), heads(v_pre), log_i, log_f)
    h = layernorm32(h, LN_EPS).transpose(0, 2, 1, 3).reshape(bsz, seqlen, M_WIDTH)
    return (jax.nn.sigmoid(o_pre.astype(jnp.float32)) * h * head_g).astype(q_pre.dtype)

def sgu_branch(z_pre, norm_g, norm_b, w_s, b_s):
    bsz, seqlen, _ = z_pre.shape
    u, v = jnp.split(jax.nn.gelu(z_pre, approximate=False), 2, axis=-1)
    v = (layernorm32(v, LN_EPS) * norm_g + norm_b).astype(z_pre.dtype)
    nb = seqlen // SGU_BLOCK
    v = v.reshape(bsz, nb, SGU_BLOCK, SGU_GROUPS, SGU_GROUP_DIM)
    chunk_id = jnp.arange(SGU_BLOCK) // CHUNK
    mask = chunk_id[:, None] >= chunk_id[None, :]
    w = jnp.where(mask, w_s, 0.0).astype(v.dtype)
    sv = jnp.einsum('gts,bnsgc->bntgc', w, v) + b_s.T[:, :, None].astype(v.dtype)
    return u * sv.reshape(bsz, seqlen, SGU_WIDTH)

def second_inputs(seed: int = 0) -> dict:
    key = jax.random.key(seed)
    ks = jax.random.split(key, 20)
    L = DEPTH

    def nrm(k, shape, scale):
        return jax.random.normal(k, shape, jnp.float32) * scale

    return {
        'x': nrm(ks[0], (BATCH, SEQ, D_MODEL), 1.0),
        'ffn1_norm_g': 1.0 + nrm(ks[1], (L, D_MODEL), 0.05),
        'ffn1_w_in': nrm(ks[2], (L, D_MODEL, 2 * D_FF), D_MODEL ** -0.5),
        'ffn1_w_out': nrm(ks[3], (L, D_FF, D_MODEL), D_FF ** -0.5),
        'mix_norm_g': 1.0 + nrm(ks[4], (L, D_MODEL), 0.05),
        'w_mix_in': nrm(ks[5], (L, D_MODEL, N_PROJ), D_MODEL ** -0.5),
        'mlstm_conv_w': nrm(ks[6], (L, CONV_K, 2 * M_WIDTH), CONV_K ** -0.5),
        'mlstm_conv_b': nrm(ks[7], (L, 2 * M_WIDTH), 0.01),
        'mlstm_b_igate': nrm(ks[8], (L, M_HEADS), 0.1),
        'mlstm_b_fgate': jnp.linspace(3.0, 6.0, M_HEADS, dtype=jnp.float32) + nrm(ks[9], (L, M_HEADS), 0.1),
        'mlstm_head_norm_g': 1.0 + nrm(ks[10], (L, M_WIDTH), 0.05),
        'sgu_norm_g': 1.0 + nrm(ks[11], (L, SGU_WIDTH), 0.05),
        'sgu_norm_b': nrm(ks[12], (L, SGU_WIDTH), 0.01),
        'sgu_w_s': nrm(ks[13], (L, SGU_GROUPS, SGU_BLOCK, SGU_BLOCK), SGU_BLOCK ** -0.5),
        'sgu_b_s': 1.0 + nrm(ks[14], (L, SGU_GROUPS, SGU_BLOCK), 0.1),
        'w_mix_out': nrm(ks[15], (L, D_MODEL, D_MODEL), D_MODEL ** -0.5),
        'ffn2_norm_g': 1.0 + nrm(ks[16], (L, D_MODEL), 0.05),
        'ffn2_w_in': nrm(ks[17], (L, D_MODEL, 2 * D_FF), D_MODEL ** -0.5),
        'ffn2_w_out': nrm(ks[18], (L, D_FF, D_MODEL), D_FF ** -0.5),
        'final_norm_g': 1.0 + nrm(ks[19], (D_MODEL,), 0.05),
    }

def second_block(x, ffn1_norm_g, ffn1_w_in, ffn1_w_out, mix_norm_g, w_mix_in, mlstm_conv_w, mlstm_conv_b,
              mlstm_b_igate, mlstm_b_fgate, mlstm_head_norm_g, sgu_norm_g, sgu_norm_b, sgu_w_s, sgu_b_s,
              w_mix_out, ffn2_norm_g, ffn2_w_in, ffn2_w_out, final_norm_g):
    split_idx = np.cumsum(PROJ_SIZES)[:-1].tolist()
    for l in range(DEPTH):
        x = x + 0.5 * swiglu(rmsnorm(x, ffn1_norm_g[l]), ffn1_w_in[l], ffn1_w_out[l])
        xn = rmsnorm(x, mix_norm_g[l])
        proj = xn @ w_mix_in[l]
        q_pre, k_pre, v_pre, o_pre, i_pre, f_pre, z_pre, gate_m, gate_s = jnp.split(proj, split_idx, axis=-1)
        h_m = mlstm_branch(q_pre, k_pre, v_pre, o_pre, i_pre, f_pre, mlstm_conv_w[l], mlstm_conv_b[l],
                           mlstm_b_igate[l], mlstm_b_fgate[l], mlstm_head_norm_g[l])
        h_s = sgu_branch(z_pre, sgu_norm_g[l], sgu_norm_b[l], sgu_w_s[l], sgu_b_s[l])
        merged = jax.nn.sigmoid(gate_m) * h_m + jax.nn.sigmoid(gate_s) * h_s
        x = x + merged @ w_mix_out[l]
        x = x + 0.5 * swiglu(rmsnorm(x, ffn2_norm_g[l]), ffn2_w_in[l], ffn2_w_out[l])
    return rmsnorm(x, final_norm_g)


def setup_inputs(seed=0):
    out = dict(first_inputs(seed))
    for name, value in second_inputs(seed + 1).items():
        if name != "x":
            out[name + "_2"] = value
    return out


def reference(
    x, c, ada_w, ada_b, norm_g, final_g, sb_w_in, sb_w_out, gla_w_in, gla_w_gate_up, gla_b_gate,
    gla_norm_g, gla_w_out, conv_w_in, conv_w, conv_b, conv_w_out, dil_w_in, dil_w_out,
    moe_w_grp, moe_b_grp, moe_w_exp, moe_b_exp, moe_w_gate, moe_w_up, moe_w_down, ffn1_norm_g_2,
    ffn1_w_in_2, ffn1_w_out_2, mix_norm_g_2, w_mix_in_2, mlstm_conv_w_2, mlstm_conv_b_2,
    mlstm_b_igate_2, mlstm_b_fgate_2, mlstm_head_norm_g_2, sgu_norm_g_2, sgu_norm_b_2,
    sgu_w_s_2, sgu_b_s_2, w_mix_out_2, ffn2_norm_g_2, ffn2_w_in_2, ffn2_w_out_2, final_norm_g_2,
):
    x = first_block(
        x, c, ada_w, ada_b, norm_g, final_g, sb_w_in, sb_w_out, gla_w_in, gla_w_gate_up,
        gla_b_gate, gla_norm_g, gla_w_out, conv_w_in, conv_w, conv_b, conv_w_out, dil_w_in,
        dil_w_out, moe_w_grp, moe_b_grp, moe_w_exp, moe_b_exp, moe_w_gate, moe_w_up, moe_w_down,
    )
    return second_block(
        x, ffn1_norm_g_2, ffn1_w_in_2, ffn1_w_out_2, mix_norm_g_2, w_mix_in_2, mlstm_conv_w_2,
        mlstm_conv_b_2, mlstm_b_igate_2, mlstm_b_fgate_2, mlstm_head_norm_g_2, sgu_norm_g_2,
        sgu_norm_b_2, sgu_w_s_2, sgu_b_s_2, w_mix_out_2, ffn2_norm_g_2, ffn2_w_in_2,
        ffn2_w_out_2, final_norm_g_2,
    )


_drawn_inputs = setup_inputs


def setup_inputs(seed=0):
    import zlib

    import numpy as np

    out = dict(_drawn_inputs(seed))
    spreads = {}
    factors = {'ada_b': 3.695,
     'norm_g': 4.145,
     'moe_b_grp': 8.0,
     'moe_b_exp': 8.0,
     'mlstm_conv_b_2': 8.0,
     'mlstm_b_igate_2': 200.0,
     'mlstm_head_norm_g_2': 4.508,
     'sgu_norm_g_2': 4.004,
     'sgu_norm_b_2': 30.099,
     'ffn2_norm_g_2': 3.111}
    for name, (base, spread) in spreads.items():
        noise = np.random.default_rng([zlib.crc32(name.encode()), seed]).standard_normal(out[name].shape)
        drawn = base * np.exp(spread * noise) if base else spread * noise
        out[name] = __import__('jax').numpy.asarray(drawn.astype(out[name].dtype))
    for name, factor in factors.items():
        out[name] = (out[name] * factor).astype(out[name].dtype)
    return out
```

```python
from contextlib import ExitStack

import concourse.bass as bass
from concourse import mybir

FP32 = mybir.dt.float32
INT32 = mybir.dt.int32
ALU = mybir.AluOpType
ACT = mybir.ActivationFunctionType
AX = mybir.AxisListType.X

P = 128
D = 1024
T = 256
NT = T // P
KD = D // P
NB = 512
RMS_EPS = 1e-6
LN_EPS = 1e-5

HEADS, DH = 16, 64
BLK = 3 * P

GROUPS, EXPERTS, FF_E = 4, 32, 512
CAP = 32
EG = P // CAP
NEG = EXPERTS // EG
ROUNDS = T // CAP
KF_E = FF_E // P

FF = 2816
NF = FF // P

MH, MD = 4, 256
CONV_K = 4
SG, SGC = 4, 256

RING_A, RING_B = 6, 4
SLOT = 4096
UNITS_PER_GROUP = KD + KF_E


class BankPlan:

    def __init__(self):
        self.uses, self.emptied, self.filled, self.turn = {}, [0] * 8, [0] * 8, 0

    def use(self, name, bank=None, fills=1):
        if bank is None:
            bank = self.turn % 8
            self.turn += 1
        self.uses[name] = (bank, self.emptied[bank], self.filled[bank])
        self.emptied[bank] += 1
        self.filled[bank] += fills


def plan_banks():
    plan = BankPlan()

    def transposes(j):
        for tt in range(NT):
            for half in range(2):
                plan.use(("T", j, tt, half))

    for j in range(4):
        plan.use(("ada", j))
    transposes(0)
    for u in range(4):
        for i in range(2):
            plan.use(("qk", u, i))
    for u in range(2):
        for tt in range(NT):
            plan.use(("v", u, tt))
    for h in range(HEADS + 2):
        if h < HEADS:
            plan.use(("z", h), bank=h % 4, fills=2)
        if h >= 2 and h % 2 == 0:
            plan.use(("o", (h - 2) // 2), bank=4 + (h // 2) % 2, fills=0)
        if h < HEADS and h % 2 == 1:
            plan.use(("ada", 4 + h // 2), bank=6 + (h // 2) % 2)
    plan.turn = 0
    for u in range(2):
        for tt in range(NT):
            plan.use(("out", u, tt))
    transposes(1)
    plan.use(("router", 0))
    plan.use(("router", 1))

    def ffn(n):
        plan.turn = 0
        for j in range(FF // 256):
            plan.use(("gate", n, j), bank=2 * (j % 2))
            plan.use(("up", n, j), bank=2 * (j % 2) + 1)
        for i in range(4):
            plan.use(("down", n, i), bank=4 + i)

    transposes(2)
    ffn(0)
    plan.turn = 0
    plan.use(("cols",))
    plan.use(("ws",))
    transposes(3)
    plan.use(("if",))
    for u in range(4):
        for i in range(2):
            plan.use(("cq", u, i))
        if u == 0:
            plan.use(("B",))
        if u == 1:
            plan.use(("uT",))
        if u == 2:
            plan.use(("Mbc", 0))
            plan.use(("Mbc", 1))
            plan.use(("Mt",))
    for u in range(2):
        for tt in range(NT):
            plan.use(("mv", u, tt))
    for u in range(4):
        for tt in range(NT):
            plan.use(("mz", u, tt))
        plan.use(("s", u))
    for u in range(2):
        for tt in range(NT):
            plan.use(("mo", u, tt))
        for h in (2 * u, 2 * u + 1):
            for tt in range(NT):
                plan.use(("num", h, tt))
    for u in range(2):
        for tt in range(NT):
            plan.use(("mgm", u, tt))
    for tt in range(NT):
        for half in range(2):
            plan.use(("sv", tt, half))
    for u in range(2):
        for tt in range(NT):
            plan.use(("mgs", u, tt))
    transposes(4)
    for u in range(2):
        for tt in range(NT):
            plan.use(("mout", u, tt))
    transposes(5)
    ffn(1)
    return plan.uses


class Chain:

    def __init__(self, engine, sem):
        self.engine, self.sem, self.count = engine, sem, 0

    def step(self, ins):
        self.count += 1
        ins.then_inc(self.sem, 1)
        return self.count

    def link(self, ins):
        self.engine.wait_ge(self.sem, self.step(ins))

    def wait(self, count):
        self.engine.wait_ge(self.sem, count)


def build_program(nc, x_in, c_in, ada_w, ada_b, norm_g, final_g, sb_w_in, sb_w_out, moe_w_grp, moe_b_grp,
                  moe_w_exp, moe_b_exp, moe_w_gate, moe_w_up, moe_w_down, ffn1_norm_g, ffn1_w_in, ffn1_w_out,
                  mix_norm_g, w_mix_in, conv_w, conv_b, b_igate, b_fgate, head_g, sgu_g, sgu_b, sgu_w_s,
                  sgu_b_s, w_mix_out, ffn2_norm_g, ffn2_w_in, ffn2_w_out, final2_g, out):
    uses = plan_banks()
    ctx = ExitStack()
    with ctx:
        def sb(name, shape, dt=FP32):
            return ctx.enter_context(nc.sbuf_tensor(name, shape, dt))

        def sem(name):
            return ctx.enter_context(nc.semaphore(name))

        ring = sb("ring", [P, RING_B * SLOT])
        x = sb("x", [P, NT, D])
        hn = sb("hn", [P, NT, D])
        hT = sb("hT", [P, KD, T])
        gain0 = sb("gain0", [P, D])
        gain1 = sb("gain1", [P, D])
        ident = sb("ident", [P, P])
        neg_ge = sb("neg_ge", [P, P])
        neg_ones = sb("neg_ones", [P, P])
        ones = sb("ones", [P, P])
        lt = sb("lt", [P, P])
        le = sb("le", [P, P])
        pick = sb("pick", [MH, MH, P])
        iota = sb("iota", [P, EXPERTS])
        iotam = sb("iotam", [P, EXPERTS])
        ccol = sb("ccol", [P, 2, KD])
        ss = sb("ss", [P, 7, NT])
        eps = sb("eps", [P, 2])
        rs = sb("rs", [P, 7, NT])
        wr = sb("wr", [P, KD, GROUPS + EXPERTS])
        rbias = sb("rbias", [P, GROUPS + EXPERTS])
        gbias = sb("gbias", [P, 2 * MH])
        wif = sb("wif", [P, KD, 2 * MH])
        posm = sb("posm", [P, NT, EXPERTS])
        gw = sb("gw", [P, NT, EXPERTS])
        maxcount = sb("maxcount", [1, 1], INT32)
        ARENA = 25856
        arena = sb("arena", [P, ARENA])
        psum = ctx.enter_context(nc.psum_tensor("psum", [P, 8, NB], FP32))

        def area(at, *shape):
            size = 1
            for n in shape:
                size *= n
            assert at + size <= ARENA
            flat = arena[:, at:at + size]
            if len(shape) == 1:
                return flat
            names = "abc"[:len(shape)]
            return flat.rearrange(f"p ({' '.join(names)}) -> p {' '.join(names)}",
                                  **{n: s for n, s in zip(names, shape)})

        ring_tail = area(0, 2, SLOT)
        modb = area(8192, 6, D)
        qkT = area(14336, 2 * KD, T)
        vtok = area(18432, NT, D)
        oT = area(20480, KD, T)
        att_az = area(22528, 2, BLK)
        att_sp = area(23296, 2, BLK)
        att_a = area(24064, 2, BLK)
        crep = area(24832, KD, P)
        m_sel = area(14336, NT, EG, CAP)
        m_wsel = area(14592, NT, EG, CAP)
        m_xT = area(14848, KD, P)
        m_wT = area(15872, NT, P)
        m_sg = area(16128, FF_E)
        m_h = area(16640, FF_E)
        m_hT = area(17152, KF_E, P)
        m_y = area(17664, D)
        yacc = area(18688, NT, D)
        gain_f = area(20736, D)
        gain_f1 = area(21760, D)
        route = area(22784, 2048)
        actT = area(0, NF, T)
        sil = area(5632, 2, NB)
        mqkT = area(0, 2 * KD, T)
        conv = area(4096, 2, NB)
        vx = area(5120, NT, MH, MD + 1)
        sig_o = area(7176, NT, D)
        zu = area(9224, NT, D)
        zv = area(11272, NT, D)
        sig_gm = area(13320, NT, D)
        hm = area(15368, NT * MH, MD + 1)
        decay = area(17424, MH, BLK)
        sdec = area(18960, 2, BLK)
        wsT = area(19728, SG, P)
        small = area(20240, 424)
        gain_mix = area(22784, D)
        gain_head = area(23808, D)
        gain_sg = area(24832, D)
        gain_sb = area(20736, D)
        gain_f2 = area(21760, D)
        spatial_stat = small[:, 144:148].rearrange("p (a n) -> p a n", a=NT)
        spatial_var = spatial_stat[:, :, 1]
        head_var = conv[:, 0, 72:80]
        cols = small[:, 0:84]
        rows84 = sb("rows84", [84, P])
        wrows = area(16896, SG, P)

        def slot_a(n):
            s = n % RING_A
            return ring[:, s * SLOT:(s + 1) * SLOT] if s < RING_B else ring_tail[:, s - RING_B, :]

        def slot_b(n):
            s = n % RING_B
            return ring[:, s * SLOT:(s + 1) * SLOT]

        bank_full = [sem(f"bank{b}_full") for b in range(8)]
        bank_free = [sem(f"bank{b}_free") for b in range(8)]
        wa_in = [sem(f"wa{s}_in") for s in range(RING_A)]
        wb_in = [sem(f"wb{s}_in") for s in range(RING_B)]
        down_used = sem("down_used")
        consts = sem("consts")
        x_in_s, c_in_s, ada_b_s, g0_s, g1_s, rt_s = (sem(n) for n in (
            "x_landed", "c_landed", "ada_b_landed", "gain0_landed", "gain1_landed", "router_landed"))
        gf_s, colrow_s, ws_s, if_s, gmix_s = (sem(n) for n in (
            "gain_f_landed", "colrows_landed", "ws_landed", "if_landed", "gain_mix_landed"))
        gf2_s, gfin_s, out_s = sem("gain_f2_landed"), sem("gain_fin_landed"), sem("out_stored")
        gsg_s = sem("gain_sg_landed")
        c_silu, c_rep = sem("c_silu"), sem("c_rep")
        x_ready = sem("x_ready")
        ss_ready = sem("ss_ready")
        rs_ready = sem("rs_ready")
        var_ready, inv_ready = sem("var_ready"), sem("inv_ready")
        hn_ready = sem("hn_ready")
        dve_s, act_s, pool_s = sem("dve_steps"), sem("act_steps"), sem("pool_steps")
        z_log, z_sp, z_spm, z_a, z_am, z_o = (sem(n) for n in (
            "att_log", "att_sp", "att_sp_masked", "att_a", "att_a_masked", "att_o"))
        r_diff, r_exp, r_sel, r_done = sem("rt_diff"), sem("rt_exp"), sem("rt_selected"), sem("rt_done")
        qk_s, zf_s, fl_s = sem("qk_silu"), sem("f_abs"), sem("f_log")
        lf_s, u_s, m_s, em_s = sem("logf"), sem("u_ready"), sem("m_ready"), sem("em_ready")
        d_s, dm_s = sem("decay_exp"), sem("decay_masked")
        vn_s, hg_s, gg_s, ws_m = sem("v_normed"), sem("gates_gained"), sem("gates_times"), sem("ws_masked")

        class Experts:

            def __init__(self, tag, credit):
                self.credit = credit
                self.used = sem(f"{tag}_used")
                self.sel, self.xa, self.xv, self.sg, self.h = (sem(f"{tag}_{n}") for n in (
                    "sel", "x_copied_act", "x_copied_dve", "silu", "hidden"))
                self.hT, self.ya, self.yv, self.acc = (sem(f"{tag}_{n}") for n in (
                    "hiddenT", "y_copied_act", "y_copied_dve", "accumulated"))
                self.x_full, self.hT_full, self.c_full = (sem(f"{tag}_{n}") for n in (
                    "x_full", "hT_full", "combined_full"))
                self.steps = sem(f"{tag}_steps")

        main, over = Experts("moe", 0), Experts("over", RING_A)
        over_in = [sem(f"over{s}_in") for s in range(RING_A)]

        def await_unit_used(eng, unit):
            kind, u = unit[0], unit[-1]
            if kind == "down":
                n = unit[1]
                if u < n_out - 1:
                    eng.wait_ge(down_used, n * (n_out - 1) + u + 1)
                else:
                    await_full(eng, ("down", n, 3))
                return
            last = {"ada": ("ada", u), "qkv": ("qk", u, 1) if u < 4 else ("v", u - 4, 1), "out": ("out", u, 1),
                    "in": ("up", unit[1], u), "mout": ("mout", u, 1)}.get(kind)
            if kind == "mix":
                i = mix_units.index(unit[1:])
                last = ("cq", i, 1) if i < 4 else {
                    "v": ("mv", u, 1), "z": ("mz", (u + 2) % 4, 1), "o": ("mo", u, 1), "gm": ("mgm", u, 1),
                    "gs": ("mgs", u, 1)}[unit[1]]
            await_full(eng, last)

        def await_units(eng, S, it, units):
            eng.wait_ge(S.used, it * UNITS_PER_GROUP + (S.credit + units))

        def bank(name):
            return psum[:, uses[name][0], :]

        def open_bank(pe, name):
            b, n, _ = uses[name]
            if n:
                pe.wait_ge(bank_free[b], n)
            return psum[:, b, :]

        def filled(ins, name):
            ins.then_inc(bank_full[uses[name][0]], 1)

        def await_full(eng, name, nth=1):
            b, _, f = uses[name]
            eng.wait_ge(bank_full[b], f + nth)
            return psum[:, b, :]

        def emptied(ins, name):
            ins.then_inc(bank_free[uses[name][0]], 1)

        def await_copied(eng, name):
            b, n, _ = uses[name]
            eng.wait_ge(bank_free[b], n + 1)

        units_a = [("ada", j) for j in range(4)] + [("qkv", j) for j in range(6)]
        units_a += [("ada", j) for j in range(4, 12)] + [("out", j) for j in range(2)]
        at_a = {u: n for n, u in enumerate(units_a)}
        NA = len(units_a)
        mix_cols = {"q": 0, "k": D, "v": 2 * D, "o": 3 * D, "z": 4 * D + 2 * MH,
                    "gm": 6 * D + 2 * MH, "gs": 7 * D + 2 * MH}
        mix_units = [("q", 0), ("q", 1), ("k", 0), ("k", 1), ("v", 0), ("v", 1), ("z", 2), ("z", 3),
                     ("z", 0), ("z", 1), ("o", 0), ("o", 1), ("gm", 0), ("gm", 1), ("gs", 0), ("gs", 1)]
        n_in, n_out = FF // 256, -(-NF // 4)
        units_b = [("in", 0, j) for j in range(n_in)] + [("down", 0, j) for j in range(n_out)]
        units_b += [("mix", *u) for u in mix_units] + [("mout", j) for j in range(2)]
        units_b += [("in", 1, j) for j in range(n_in)] + [("down", 1, j) for j in range(n_out)]
        at_b = {u: n for n, u in enumerate(units_b)}

        ada_v = ada_w[0].rearrange("(p k) n -> p k n", k=KD)
        sbin_v = sb_w_in[0].rearrange("(k p) n -> p k n", p=P)
        sbout_v = sb_w_out[0].rearrange("(k p) n -> p k n", p=P)
        mixin_v = w_mix_in[0].rearrange("(k p) n -> p k n", p=P)
        mixout_v = w_mix_out[0].rearrange("(k p) n -> p k n", p=P)
        ffin_v = [w[0].rearrange("(k p) n -> p k n", p=P) for w in (ffn1_w_in, ffn2_w_in)]
        ffout_v = [w[0].rearrange("(k p) n -> p k n", p=P) for w in (ffn1_w_out, ffn2_w_out)]
        gate_v = moe_w_gate[0].rearrange("e (k p) n -> p k e n", p=P)
        up_v = moe_w_up[0].rearrange("e (k p) n -> p k e n", p=P)
        down_v = moe_w_down[0].rearrange("e (k p) n -> p k e n", p=P)

        def by_k(flat, k=KD):
            return flat.rearrange("p (k n) -> p k n", k=k)

        block = ctx.enter_context(nc.Block())

        @block.sync
        def _(sp):
            def load_k(slot, view, cols, landed):
                dst = by_k(slot)
                for a in range(2):
                    sp.dma_start(dst[:, 4 * a:4 * a + 4, :], view[:, 4 * a:4 * a + 4, cols:cols + NB])\
                      .then_inc(landed, 16)

            for n, (kind, j) in enumerate(units_a):
                if n >= RING_A:
                    await_unit_used(sp, units_a[n - RING_A])
                view = {"ada": ada_v, "qkv": sbin_v, "out": sbout_v}[kind]
                load_k(slot_a(n), view, j * NB, wa_in[n % RING_A])

            def expert_units(first, g, it, S, landed):
                for u in range(UNITS_PER_GROUP):
                    n = first + u
                    if S is main and isinstance(it, int) and u < RING_A:
                        await_unit_used(sp, units_a[NA - RING_A + u])
                    else:
                        sp.wait_ge(S.used, it * UNITS_PER_GROUP + (u + 1 - RING_A + S.credit))
                    dst = slot_a(n)
                    s = landed[n % RING_A]
                    if u < KD:
                        dst = dst.rearrange("p (w e n) -> p w e n", w=2, e=EG)
                        for w, view in enumerate((gate_v, up_v)):
                            sp.dma_start(dst[:, w], view[:, u, bass.ds(g * EG, EG), :]).then_inc(s, 16)
                    else:
                        dst = dst.rearrange("p (e n) -> p e n", e=EG)
                        for a in range(2):
                            sp.dma_start(dst[:, 2 * a:2 * a + 2, :],
                                         down_v[:, u - KD, bass.ds(g * EG + 2 * a, 2), :]).then_inc(s, 16)

            expert_units(NA, 0, 0, main, wa_in)
            with sp.Fori(1, NEG) as g:
                expert_units(NA, g, g, main, wa_in)
            sp.wait_ge(r_done, 1)
            longest = sp.value_load(maxcount[:], min_val=0, max_val=T)
            with sp.If(longest > CAP):
                sp.wait_ge(main.used, NEG * UNITS_PER_GROUP)
                with sp.Fori(0, ROUNDS - 1) as r:
                    with sp.Fori(0, NEG) as g:
                        expert_units(0, g, r * NEG + g, over, over_in)
                sp.wait_ge(over.used, RING_A + (ROUNDS - 1) * NEG * UNITS_PER_GROUP)
            sp.end_ifs()

            done_a = NA + NEG * UNITS_PER_GROUP
            for n, unit in enumerate(units_b):
                if n < RING_B:
                    last = max(m for m in range(done_a) if m % RING_A == n)
                    sp.wait_ge(main.used, last - NA + 1)
                else:
                    await_unit_used(sp, units_b[n - RING_B])
                dst, s = slot_b(n), wb_in[n % RING_B]
                if unit[0] == "in":
                    view, j = ffin_v[unit[1]], unit[2]
                    dst = dst.rearrange("p (k w n) -> p k w n", k=KD, w=2)
                    for w in range(2):
                        lo = w * FF + 256 * j
                        sp.dma_start(dst[:, :, w, :], view[:, :, lo:lo + 256]).then_inc(s, 16)
                elif unit[0] == "down":
                    view, j = ffout_v[unit[1]], unit[2]
                    k = min(4, NF - 4 * j)
                    dst = by_k(dst, 4)
                    for a in range(2):
                        sp.dma_start(dst[:, a * k // 2:(a + 1) * k // 2, :],
                                     view[:, 4 * j + a * k // 2:4 * j + (a + 1) * k // 2, :]).then_inc(s, 16)
                elif unit[0] == "mix":
                    load_k(dst, mixin_v, mix_cols[unit[1]] + NB * unit[2], s)
                else:
                    load_k(dst, mixout_v, NB * unit[1], s)

        @block.gpsimd
        def _(pool):
            chain = Chain(pool, pool_s)
            g = nc.gpsimd
            for t, v in ((ident, 0.0), (neg_ge, -1.0), (lt, 1.0), (le, 1.0), (pick, 0.0)):
                last = chain.step(g.memset(t[:], v))
            g.memset(neg_ones[:], -1.0).then_inc(consts, 1)
            g.memset(ones[:], 1.0).then_inc(consts, 1)
            g.memset(eps[:, 0:1], RMS_EPS).then_inc(consts, 1)
            g.memset(eps[:, 1:2], LN_EPS).then_inc(consts, 1)
            chain.wait(last)
            g.affine_select(out=ident[:], in_=ident[:], compare_op=ALU.not_equal, fill=1.0, base=0,
                            pattern=[[-1, P]], channel_multiplier=1).then_inc(consts, 1)
            g.affine_select(out=neg_ge[:], in_=neg_ge[:], compare_op=ALU.is_ge, fill=0.0, base=0,
                            pattern=[[-1, P]], channel_multiplier=1).then_inc(consts, 1)
            g.affine_select(out=lt[:], in_=lt[:], compare_op=ALU.is_gt, fill=0.0, base=0,
                            pattern=[[1, P]], channel_multiplier=-1).then_inc(consts, 1)
            g.affine_select(out=le[:], in_=le[:], compare_op=ALU.is_ge, fill=0.0, base=0,
                            pattern=[[1, P]], channel_multiplier=-1).then_inc(consts, 1)
            g.affine_select(out=pick[:], in_=pick[:], compare_op=ALU.not_equal, fill=1.0, base=0,
                            pattern=[[-1, MH], [0, P]], channel_multiplier=1).then_inc(consts, 1)
            g.iota(iota[:], pattern=[[1, EXPERTS]], base=0, channel_multiplier=0,
                   allow_small_or_imprecise_dtypes=True).then_inc(consts, 1)
            g.iota(iotam[:], pattern=[[1, EXPERTS]], base=-64, channel_multiplier=0,
                   allow_small_or_imprecise_dtypes=True).then_inc(consts, 1)

            def diag(t):
                return t.rearrange("p (b q) -> p b q", b=3)[:, 0::2, :]

            for h in range(HEADS + 1):
                if h < HEADS:
                    pool.wait_ge(z_sp, h + 1)
                    m = diag(att_sp[:, h % 2, :])
                    g.affine_select(out=m, in_=m, compare_op=ALU.is_gt, fill=0.0, base=0,
                                    pattern=[[0, 2], [1, P]], channel_multiplier=-1).then_inc(z_spm, 1)
                if h >= 1:
                    pool.wait_ge(z_a, h)
                    m = diag(att_a[:, (h - 1) % 2, :])
                    g.affine_select(out=m, in_=m, compare_op=ALU.is_gt, fill=0.0, base=0,
                                    pattern=[[0, 2], [1, P]], channel_multiplier=-1).then_inc(z_am, 1)

            for h in range(MH):
                pool.wait_ge(d_s, h + 1)
                m = diag(decay[:, h, :])
                g.affine_select(out=m, in_=m, compare_op=ALU.is_ge, fill=0.0, base=0,
                                pattern=[[0, 2], [1, P]], channel_multiplier=-1).then_inc(dm_s, 1)
            for tt in range(NT):
                for u in range(2):
                    await_copied(pool, ("mo", u, tt))
                    await_copied(pool, ("mgm", u, tt))
                g.tensor_tensor(out=sig_gm[:, tt, :], in0=sig_gm[:, tt, :], in1=sig_o[:, tt, :], op=ALU.mult)\
                 .then_inc(gg_s, 1)
            pool.wait_ge(gmix_s, 32)
            for tt in range(NT):
                pool.wait_ge(gg_s, tt + 1)
                g.tensor_tensor(out=sig_gm[:, tt, :], in0=sig_gm[:, tt, :], in1=gain_head, op=ALU.mult)\
                 .then_inc(hg_s, 1)

        @block.scalar
        def _(act):
            a = nc.scalar
            chain = Chain(act, act_s)

            def row(v):
                return v.partition_broadcast(P)

            act.dma_start(ccol[:, 0, :], c_in[0].rearrange("(p k) -> p k", k=KD)).then_inc(c_in_s, 16)
            act.dma_start(x[:], x_in[0].rearrange("(t p) d -> p t d", p=P)).then_inc(x_in_s, 16)
            act.dma_start(modb.rearrange("p a d -> p (a d)"), row(ada_b[0])).then_inc(ada_b_s, 16)
            act.dma_start(gain0[:], row(norm_g[0, 0])).then_inc(g0_s, 16)
            act.dma_start(gain1[:], row(norm_g[0, 1])).then_inc(g1_s, 16)
            with nc.allow_non_contiguous_dma(reason="36 router columns"):
                act.dma_start(wr[:, :, 0:GROUPS], moe_w_grp[0].rearrange("(k p) n -> p k n", p=P)).then_inc(rt_s, 16)
                act.dma_start(wr[:, :, GROUPS:], moe_w_exp[0].rearrange("(k p) n -> p k n", p=P)).then_inc(rt_s, 16)
                act.dma_start(wif[:], mixin_v[:, :, 4 * D:4 * D + 2 * MH]).then_inc(if_s, 16)
            act.dma_start(rbias[:, 0:GROUPS], row(moe_b_grp[0])).then_inc(rt_s, 16)
            act.dma_start(rbias[:, GROUPS:], row(moe_b_exp[0])).then_inc(rt_s, 16)
            act.dma_start(gbias[:, 0:MH], row(b_igate[0])).then_inc(if_s, 16)
            act.dma_start(gbias[:, MH:], row(b_fgate[0])).then_inc(if_s, 16)
            act.dma_start(rows84[0:64, :], conv_w[0].rearrange("j (f p) -> (j f) p", p=P)).then_inc(colrow_s, 16)
            act.dma_start(rows84[64:80, :], conv_b[0].rearrange("(f p) -> f p", p=P)).then_inc(colrow_s, 16)
            act.dma_start(rows84[80:84, :], sgu_b_s[0]).then_inc(colrow_s, 16)

            act.wait_ge(c_in_s, 16)
            a.activation(ccol[:, 1, :], ccol[:, 0, :], ACT.Silu).then_inc(c_silu, 1)

            def squares(i):
                if i == 0:
                    act.wait_ge(x_in_s, 16)
                for tt in range(NT):
                    if 1 <= i <= 3:
                        act.wait_ge(x_ready, NT * (i - 1) + tt + 1)
                    elif i:
                        await_copied(act, {4: ("down", 0, 2 * tt + 1), 5: ("mout", 1, tt), 6: ("down", 1, 2 * tt + 1)}[i])
                    a.activation(hn[:, tt, :], x[:, tt, :], ACT.Square, scale=D ** -0.5, accum_out=ss[:, i, tt:tt + 1])\
                     .then_inc(ss_ready, 1)
                act.wait_ge(ss_ready, NT * (i + 1))
                a.activation(rs[:, i, :], ss[:, i, :], ACT.Sqrt, bias=eps[:, 0:1]).then_inc(rs_ready, 1)

            def root_of_variance(n, var):
                act.wait_ge(var_ready, n + 1)
                a.activation(var, var, ACT.Sqrt, bias=eps[:, 1:2]).then_inc(inv_ready, 1)

            def transposed(j):
                for half in range(2):
                    b = await_full(act, ("T", j, 0, half))
                    emptied(a.activation(hT[:, 4 * half:4 * half + 4, 0:P], by_k(b, 4), ACT.Copy),
                            ("T", j, 0, half))

            act.wait_ge(consts, 11)
            squares(0)
            transposed(0)
            for u in range(4):
                b = await_full(act, ("qk", u, 0))
                emptied(a.activation(qkT[:, 4 * u:4 * u + 2, :], by_k(b, 2), ACT.Copy,
                                     scale=DH ** -0.5 if u < 2 else 1.0), ("qk", u, 0))
            for h in range(HEADS + 1):
                if h < HEADS:
                    s = att_az[:, h % 2, :]
                    b = await_full(act, ("z", h))
                    if h >= 2:
                        act.wait_ge(z_sp, h - 1)
                    chain.link(a.activation(s, b[:, 0:BLK], ACT.Abs))
                    chain.link(a.activation(s, s, ACT.Exp, scale=-1.0))
                    a.activation(s, s, ACT.Ln, bias=1.0).then_inc(z_log, 1)
                if h >= 1:
                    g = h - 1
                    await_copied(act, ("z", g))
                    w = att_a[:, g % 2, :]
                    a.activation(w, w, ACT.Exp).then_inc(z_a, 1)
            act.wait_ge(z_o, HEADS)
            await_copied(act, ("out", 1, 1))
            act.dma_start(gain_f, row(final_g)).then_inc(gf_s, 16)
            act.dma_start(gain_f1, row(ffn1_norm_g[0])).then_inc(gf_s, 16)
            squares(1)
            transposed(1)
            act.wait_ge(r_diff, 1)
            a.activation(route[:, 0:8], route[:, 0:8], ACT.Exp).then_inc(r_exp, 1)
            act.wait_ge(r_diff, 2)
            a.activation(route[:, 64:128], route[:, 64:128], ACT.Exp).then_inc(r_exp, 1)

            def expert_copies(it, S):
                act.wait_ge(S.x_full, it + 1)
                a.activation(m_xT[:, 0:4, :], by_k(psum[:, 0, :], 4), ACT.Copy).then_inc(S.xa, 1)
                await_units(act, S, it, KD)
                a.activation(m_sg, psum[:, 4, :], ACT.Silu).then_inc(S.sg, 1)
                act.wait_ge(S.hT_full, it + 1)
                a.activation(m_hT, by_k(psum[:, 2, :], 4), ACT.Copy).then_inc(S.hT, 1)
                await_units(act, S, it, UNITS_PER_GROUP)
                a.activation(m_y[:, 0:NB], psum[:, 6, :], ACT.Copy).then_inc(S.ya, 1)

            with act.Fori(0, NEG) as g:
                expert_copies(g, main)
            act.wait_ge(r_done, 1)
            longest = act.value_load(maxcount[:], min_val=0, max_val=T)
            with act.If(longest > CAP):
                with act.Fori(0, ROUNDS - 1) as r:
                    with act.Fori(0, NEG) as g:
                        expert_copies(r * NEG + g, over)
            act.end_ifs()

            squares(2)
            squares(3)
            act.dma_start(gain_mix, row(mix_norm_g[0])).then_inc(gmix_s, 16)
            act.dma_start(gain_head, row(head_g[0])).then_inc(gmix_s, 16)
            act.dma_start(gain_sg, row(sgu_g[0])).then_inc(gsg_s, 16)
            act.dma_start(gain_sb, row(sgu_b[0])).then_inc(gsg_s, 16)
            act.dma_start(gain0[:], row(final2_g)).then_inc(gfin_s, 16)
            transposed(2)

            def ffn(n):
                for j in range(n_in):
                    b = await_full(act, ("gate", n, j))
                    if j >= 2:
                        await_copied(act, ("up", n, j - 2))
                    ins = a.activation(sil[:, j % 2, :], b, ACT.Silu)
                    emptied(ins, ("gate", n, j))
                    if j == 0 and n == 0:
                        act.dma_start(gain_f2, row(ffn2_norm_g[0])).then_inc(gf2_s, 16)

            ffn(0)
            for i in range(4):
                await_copied(act, ("down", 0, i))
            act.dma_start(wrows, sgu_w_s[0].rearrange("g t s -> t g s")).then_inc(ws_s, 16)
            squares(4)
            b = await_full(act, ("cols",))
            emptied(a.activation(cols, b[:, 0:84], ACT.Copy), ("cols",))
            b = await_full(act, ("ws",))
            emptied(a.activation(wsT, by_k(b, 4), ACT.Copy), ("ws",))
            transposed(3)
            act.wait_ge(zf_s, 1)
            fabs = small[:, 96:104]
            chain.link(a.activation(fabs, fabs, ACT.Exp, scale=-1.0))
            a.activation(fabs, fabs, ACT.Ln, bias=1.0).then_inc(fl_s, 1)

            def qk_silu(n):
                await_copied(act, ("cq", n // 2, n % 2))
                a.activation(mqkT[:, 2 * n:2 * n + 2, :], by_k(conv[:, n % 2, :], 2), ACT.Silu).then_inc(qk_s, 1)

            for n in range(8):
                qk_silu(n)
            for i in range(2):
                await_copied(act, ("Mbc", i))
                for h in (2 * i, 2 * i + 1):
                    a.activation(decay[:, h, :], decay[:, h, :], ACT.Exp, scale=-1.0).then_inc(d_s, 1)
            await_copied(act, ("Mt",))
            a.activation(small[:, 160:168], small[:, 160:168], ACT.Exp, scale=-1.0).then_inc(em_s, 1)
            for u in range(2):
                b = await_full(act, ("mv", u, 0))
                emptied(a.activation(vx[:, 0, 2 * u:2 * u + 2, 0:MD], by_k(b, 2), ACT.Copy), ("mv", u, 0))
            for u in range(4):
                dst = zv if u < 2 else zu
                for tt in range(NT):
                    b = await_full(act, ("mz", u, tt))
                    emptied(a.activation(dst[:, tt, NB * (u % 2):NB * (u % 2) + NB], b, ACT.Gelu), ("mz", u, tt))
            root_of_variance(0, spatial_var)
            for u in range(2):
                for tt in range(NT):
                    b = await_full(act, ("mo", u, tt))
                    emptied(a.activation(sig_o[:, tt, NB * u:NB * u + NB], b, ACT.Sigmoid), ("mo", u, tt))
                for h in (2 * u, 2 * u + 1):
                    for tt in range(NT):
                        b = await_full(act, ("num", h, tt))
                        emptied(a.activation(hm[:, 2 * h + tt, :], b[:, 0:MD + 1], ACT.Copy), ("num", h, tt))
            for u in range(2):
                for tt in range(NT):
                    b = await_full(act, ("mgm", u, tt))
                    emptied(a.activation(sig_gm[:, tt, NB * u:NB * u + NB], b, ACT.Sigmoid), ("mgm", u, tt))
                if u == 0:
                    root_of_variance(1, head_var)
            for u in range(2):
                for tt in range(NT):
                    b = await_full(act, ("mgs", u, tt))
                    emptied(a.activation(zv[:, tt, NB * u:NB * u + NB], b, ACT.Sigmoid), ("mgs", u, tt))
            transposed(4)
            squares(5)
            transposed(5)
            ffn(1)
            squares(6)
            for tt in range(NT):
                act.wait_ge(hn_ready, 6 * NT + tt + 1)
                act.dma_start(out[0, tt * P:(tt + 1) * P, :], hn[:, tt, :]).then_inc(out_s, 16)
            act.wait_ge(out_s, 16 * NT)

        @block.vector
        def _(dve):
            v = nc.vector
            chain = Chain(dve, dve_s)
            link = chain.link

            def norm(i, gain, shift=None, dst=hn, ready=None):
                dve.wait_ge(rs_ready, i + 1)
                link(v.reciprocal(rs[:, i, :], rs[:, i, :]))
                for tt in range(NT):
                    ins = v.scalar_tensor_tensor(dst[:, tt, :], x[:, tt, :], rs[:, i, tt:tt + 1], gain,
                                                 ALU.mult, ALU.mult)
                    if shift is not None:
                        link(ins)
                        ins = v.tensor_tensor(dst[:, tt, :], dst[:, tt, :], shift, ALU.add)
                    ins.then_inc(hn_ready if ready is None else ready, 1)

            def transposed(j):
                for half in range(2):
                    b = await_full(dve, ("T", j, 1, half))
                    emptied(v.tensor_copy(hT[:, 4 * half:4 * half + 4, P:T], by_k(b, 4)), ("T", j, 1, half))

            dve.wait_ge(c_silu, 1)
            v.tensor_copy(crep, ccol[:, 1, :].unsqueeze(2).to_broadcast([P, KD, P])).then_inc(c_rep, 1)

            def ada(j):
                b = await_full(dve, ("ada", j))
                part = modb[:, j // 2, NB * (j % 2):NB * (j % 2) + NB]
                emptied(v.tensor_tensor(part, b, part, ALU.add), ("ada", j))
                await_copied(dve, ("ada", j))

            dve.wait_ge(ada_b_s, 16)
            for j in range(4):
                ada(j)
            dve.wait_ge(g0_s, 16)
            link(v.scalar_tensor_tensor(modb[:, 1, :], modb[:, 1, :], 1.0, gain0[:], ALU.add, ALU.mult))
            norm(0, modb[:, 1, :], modb[:, 0, :])
            transposed(0)
            for u in range(4):
                b = await_full(dve, ("qk", u, 1))
                emptied(v.tensor_scalar(qkT[:, 4 * u + 2:4 * u + 4, :], by_k(b, 2),
                                        DH ** -0.5 if u < 2 else 1.0, None, ALU.mult), ("qk", u, 1))
            for u in range(2):
                for tt in range(NT):
                    b = await_full(dve, ("v", u, tt))
                    emptied(v.tensor_copy(vtok[:, tt, NB * u:NB * u + NB], b), ("v", u, tt))

            def softplus_head(h):
                b = bank(("z", h))
                dve.wait_ge(z_log, h + 1)
                if h >= 2:
                    await_full(dve, ("z", h - 2), 2)
                v.scalar_tensor_tensor(att_sp[:, h % 2, :], b[:, 0:BLK], 0.0, att_az[:, h % 2, :],
                                       ALU.max, ALU.add).then_inc(z_sp, 1)

            for h in range(HEADS + 4):
                if 1 <= h <= HEADS:
                    softplus_head(h - 1)
                    if h % 2 == 0:
                        ada(4 + h // 2 - 1)
                if 2 <= h <= HEADS + 1:
                    g = h - 2
                    b = await_full(dve, ("z", g), 2)
                    if g >= 2:
                        dve.wait_ge(z_o, g - 1)
                    emptied(v.tensor_scalar(att_a[:, g % 2, :], b[:, 0:BLK], 0.0, None, ALU.min), ("z", g))
                if h >= 4 and h % 2 == 0:
                    p = h // 2 - 2
                    b = bank(("o", p))
                    dve.wait_ge(z_o, 2 * p + 2)
                    emptied(v.tensor_copy(oT[:, p, :], b[:, 0:T]), ("o", p))
            dve.wait_ge(g1_s, 16)
            link(v.scalar_tensor_tensor(modb[:, 4, :], modb[:, 4, :], 1.0, gain1[:], ALU.add, ALU.mult))
            for u in range(2):
                for tt in range(NT):
                    b = await_full(dve, ("out", u, tt))
                    ins = v.tensor_tensor(hT[:, 4 * tt:4 * tt + 2, :], by_k(b, 2),
                                          by_k(modb[:, 2, NB * u:NB * u + NB], 2), ALU.mult)
                    emptied(ins, ("out", u, tt))
                    await_copied(dve, ("out", u, tt))
                    part = x[:, tt, NB * u:NB * u + NB]
                    ins = v.tensor_tensor(part, part, hT[:, 4 * tt:4 * tt + 2, :].rearrange("p a n -> p (a n)"), ALU.add)
                    if u == 1:
                        ins.then_inc(x_ready, 1)
            norm(1, modb[:, 4, :], modb[:, 3, :])
            transposed(1)

            def rt(at, *shape):
                size = 1
                for n in shape:
                    size *= n
                flat = route[:, at:at + size]
                return flat if len(shape) == 1 else flat.rearrange("p (a b) -> p a b", a=shape[0])

            gl_e = rt(0, NT, GROUPS)
            ex = rt(64, NT, EXPERTS)
            logit = rt(128, NT, 36)
            gl, el = logit[:, :, 0:GROUPS], logit[:, :, GROUPS:]
            ohg, t4, negm = rt(208, NT, GROUPS), rt(216, NT, GROUPS), rt(224, NT, GROUPS)
            one_of = rt(240, NT, EXPERTS)
            pm, t32 = rt(304, NT, EXPERTS), rt(368, NT, EXPERTS)
            oh1, oh2, chosen = rt(432, NT, EXPERTS), rt(496, NT, EXPERTS), rt(560, NT, EXPERTS)
            gmax, gsum, emax, esum, idx, p1, p2, den = (rt(640 + 4 * n, NT) for n in range(8))
            cmax = rt(700, 1)

            def wide(s, n):
                return s.unsqueeze(2).to_broadcast([P, NT, n])

            def wide8(s):
                return s.unsqueeze(3).to_broadcast([P, NT, GROUPS, EXPERTS // GROUPS])

            def by_group(s):
                return s.rearrange("p a (g e) -> p a g e", g=GROUPS)

            dve.wait_ge(rt_s, 64)
            b = await_full(dve, ("router", 0))
            ins = v.tensor_tensor(logit, b[:, 0:P].rearrange("p (a n) -> p a n", a=NT)[:, :, 0:36],
                                  rbias[:].unsqueeze(1).to_broadcast([P, NT, 36]), ALU.add)
            emptied(ins, ("router", 0))
            await_copied(dve, ("router", 0))

            def first_max(dst, src, top, n, tmp):
                link(v.tensor_reduce(top, src, AX, ALU.max))
                link(v.tensor_tensor(tmp, src, wide(top, n), ALU.is_equal))
                link(v.tensor_tensor(tmp, tmp, iotam[:, 0:n].unsqueeze(1).to_broadcast([P, NT, n]), ALU.mult))
                link(v.tensor_reduce(idx, tmp, AX, ALU.min))
                link(v.tensor_tensor(dst, iotam[:, 0:n].unsqueeze(1).to_broadcast([P, NT, n]), wide(idx, n), ALU.is_equal))

            dve.wait_ge(consts, 11)
            first_max(ohg, gl, gmax, GROUPS, t4)
            v.tensor_tensor(gl_e, gl, wide(gmax, GROUPS), ALU.subtract).then_inc(r_diff, 1)
            link(v.tensor_scalar(t4, ohg, -1.0, None, ALU.add))
            link(v.tensor_scalar(negm, t4, 1e30, None, ALU.mult))
            link(v.tensor_tensor(by_group(t32), by_group(el), wide8(negm), ALU.add))
            link(v.tensor_reduce(emax, t32, AX, ALU.max))
            v.tensor_tensor(ex, t32, wide(emax, EXPERTS), ALU.subtract).then_inc(r_diff, 1)
            dve.wait_ge(r_exp, 1)
            link(v.tensor_reduce(gsum, gl_e, AX, ALU.add))
            dve.wait_ge(r_exp, 2)
            link(v.tensor_reduce(esum, ex, AX, ALU.add))
            link(v.reciprocal(esum, esum))
            link(v.tensor_tensor(one_of, ex, wide(esum, EXPERTS), ALU.mult))
            link(v.tensor_tensor(by_group(pm), by_group(one_of), wide8(t4), ALU.add))
            first_max(oh1, pm, p1, EXPERTS, t32)
            link(v.scalar_tensor_tensor(pm, oh1, -4.0, pm, ALU.mult, ALU.add))
            first_max(oh2, pm, p2, EXPERTS, t32)
            v.tensor_tensor(chosen, oh1, oh2, ALU.add).then_inc(r_sel, 1)
            link(v.tensor_tensor(den, p1, p2, ALU.add))
            link(v.tensor_tensor(den, den, gsum, ALU.mult))
            link(v.reciprocal(den, den))
            link(v.tensor_tensor(p1, p1, den, ALU.mult))
            link(v.tensor_tensor(p2, p2, den, ALU.mult))
            link(v.tensor_tensor(gw[:], oh1, wide(p1, EXPERTS), ALU.mult))
            link(v.tensor_tensor(t32, oh2, wide(p2, EXPERTS), ALU.mult))
            link(v.tensor_tensor(gw[:], gw[:], t32, ALU.add))
            link(v.memset(yacc, 0.0))
            b = await_full(dve, ("router", 1))
            dve.wait_ge(r_sel, 1)
            link(v.tensor_reduce(cmax[0:1, :], b[0:1, 64:96], AX, ALU.max))
            v.tensor_copy(maxcount[:], cmax[0:1, :]).then_inc(r_done, 1)
            ins = v.scalar_tensor_tensor(posm[:], b[:, 0:64].rearrange("p (a n) -> p a n", a=NT), 1.0, chosen,
                                         ALU.add, ALU.mult)
            emptied(ins, ("router", 1))
            await_copied(dve, ("router", 1))
            link(v.tensor_scalar(posm[:], posm[:], -1.0, None, ALU.add))

            def expert_steps(g, it, S, steps):
                def per_slot(t):
                    return t[:, :, bass.ds(g * EG, EG)].unsqueeze(3).to_broadcast([P, NT, EG, CAP])

                if S is over:
                    dve.wait_ge(S.steps, steps - 1)
                slots = iota[:, 0:CAP].unsqueeze(1).unsqueeze(1).to_broadcast([P, NT, EG, CAP])
                v.tensor_tensor(m_sel, slots, per_slot(posm), ALU.is_equal).then_inc(S.steps, 1)
                dve.wait_ge(S.steps, steps)
                v.tensor_tensor(m_wsel, m_sel, per_slot(gw), ALU.mult).then_inc(S.sel, 1)
                dve.wait_ge(S.x_full, it + 1)
                v.tensor_copy(m_xT[:, 4:8, :], by_k(psum[:, 1, :], 4))
                v.tensor_copy(m_wT, psum[:, 3, 0:T].rearrange("p (a n) -> p a n", a=NT)).then_inc(S.xv, 1)
                dve.wait_ge(S.sg, it + 1)
                v.tensor_tensor(m_h, m_sg, psum[:, 5, :], ALU.mult).then_inc(S.h, 1)
                await_units(dve, S, it, UNITS_PER_GROUP)
                v.tensor_copy(m_y[:, NB:D], psum[:, 7, :]).then_inc(S.yv, 1)
                dve.wait_ge(S.c_full, it + 1)
                for tt in range(NT):
                    for half in range(2):
                        part = yacc[:, tt, NB * half:NB * half + NB]
                        last = v.tensor_tensor(part, part, psum[:, 2 * tt + half, :], ALU.add)
                last.then_inc(S.acc, 1)
                dve.wait_ge(S.acc, it + 2)

            dve.sem_inc(main.acc, 1)
            with dve.Fori(0, NEG) as g:
                expert_steps(g, g, main, g + 1)
            longest = dve.value_load(maxcount[:], min_val=0, max_val=T)
            with dve.If(longest > CAP):
                dve.sem_inc(over.acc, 1)
                with dve.Fori(0, ROUNDS - 1) as r:
                    v.tensor_scalar(posm[:], posm[:], float(-CAP), None, ALU.add).then_inc(over.steps, 1)
                    with dve.Fori(0, NEG) as g:
                        expert_steps(g, r * NEG + g, over, r * (NEG + 1) + g + 2)
            dve.end_ifs()

            for tt in range(NT):
                link(v.tensor_tensor(yacc[:, tt, :], yacc[:, tt, :], modb[:, 5, :], ALU.mult))
                v.tensor_tensor(x[:, tt, :], x[:, tt, :], yacc[:, tt, :], ALU.add).then_inc(x_ready, 1)
            dve.wait_ge(gf_s, 32)
            norm(2, gain_f, dst=x, ready=x_ready)
            norm(3, gain_f1)
            transposed(2)

            def ffn(n):
                for j in range(n_in):
                    await_copied(dve, ("gate", n, j))
                    b = await_full(dve, ("up", n, j))
                    ins = v.tensor_tensor(actT[:, 2 * j:2 * j + 2, :], by_k(sil[:, j % 2, :], 2), by_k(b, 2), ALU.mult)
                    emptied(ins, ("up", n, j))
                for tt in range(NT):
                    for half in range(2):
                        name = ("down", n, 2 * tt + half)
                        b = await_full(dve, name)
                        part = x[:, tt, NB * half:NB * half + NB]
                        emptied(v.scalar_tensor_tensor(part, b, 0.5, part, ALU.mult, ALU.add), name)

            ffn(0)
            dve.wait_ge(gmix_s, 32)
            norm(4, gain_mix)
            transposed(3)
            await_copied(dve, ("ws",))
            v.memset(wsT[64:P, :, 0:64], 0.0).then_inc(ws_m, 1)

            fabs = small[:, 96:104]
            gates = small[:, 104:120].rearrange("p (a n) -> p a n", a=NT)
            fabs3 = fabs.rearrange("p (a n) -> p a n", a=NT)
            lf = small[:, 120:128].rearrange("p (a n) -> p a n", a=NT)
            u8 = small[:, 128:136].rearrange("p (a n) -> p a n", a=NT)
            b8 = small[:, 136:144].rearrange("p (a n) -> p a n", a=NT)
            m8 = small[:, 160:168].rearrange("p (a n) -> p a n", a=NT)
            uT = small[0:MH, 168:168 + T]
            dve.wait_ge(if_s, 48)
            b = await_full(dve, ("if",))
            ins = v.tensor_tensor(gates, b[:, 0:16].rearrange("p (a n) -> p a n", a=NT),
                                  gbias[:].unsqueeze(1).to_broadcast([P, NT, 2 * MH]), ALU.add)
            emptied(ins, ("if",))
            await_copied(dve, ("if",))
            v.scalar_tensor_tensor(fabs3, gates[:, :, MH:], -1.0, gates[:, :, MH:], ALU.mult, ALU.max).then_inc(zf_s, 1)

            def conv_tile(n):
                u, i = n // 2, n % 2
                b = await_full(dve, ("cq", u, i))
                if n >= 2:
                    dve.wait_ge(qk_s, n - 1)
                dst = conv[:, n % 2, :]
                for k in range(CONV_K):
                    tap = CONV_K - 1 - k
                    for f in range(2):
                        ft = 2 * n + f
                        w = cols[:, tap * 16 + ft:tap * 16 + ft + 1]
                        o, s = dst[:, T * f:T * f + T], b[:, T * f:T * f + T]
                        if k == 0:
                            ins = v.tensor_scalar(o, s, w, cols[:, 64 + ft:65 + ft], ALU.mult, ALU.add)
                        else:
                            ins = v.scalar_tensor_tensor(o[:, k:T], s[:, 0:T - k], w, o[:, k:T], ALU.mult, ALU.add)
                        if f == 0:
                            continue
                        if k < CONV_K - 1:
                            link(ins)
                        else:
                            emptied(ins, ("cq", u, i))

            await_copied(dve, ("cols",))
            conv_tile(0)
            dve.wait_ge(fl_s, 1)
            v.scalar_tensor_tensor(lf, gates[:, :, MH:], 0.0, fabs3, ALU.min, ALU.subtract).then_inc(lf_s, 1)
            conv_tile(1)
            b = await_full(dve, ("B",))
            emptied(v.tensor_copy(b8, b[:, 0:8].rearrange("p (a n) -> p a n", a=NT)), ("B",))
            await_copied(dve, ("B",))
            ins = v.tensor_tensor(u8, gates[:, :, 0:MH], b8, ALU.subtract)
            ins.then_inc(u_s, 1)
            conv_tile(2)
            conv_tile(3)
            b = await_full(dve, ("uT",))
            emptied(v.tensor_copy(uT, b[0:MH, 0:T]), ("uT",))
            await_copied(dve, ("uT",))
            v.tensor_tensor_scan(sdec[0:MH, 0, 0:T], uT, uT, 0.0, ALU.max, ALU.max).then_inc(m_s, 1)
            conv_tile(4)
            conv_tile(5)
            b = await_full(dve, ("Mt",))
            ins = v.tensor_tensor(m8, b8, b[:, 0:8].rearrange("p (a n) -> p a n", a=NT), ALU.add)
            emptied(ins, ("Mt",))
            for i in range(2):
                b = await_full(dve, ("Mbc", i))
                for h in (2 * i, 2 * i + 1):
                    m = b[:, T * (h % 2):T * (h % 2) + T]
                    v.tensor_scalar(decay[:, h, 0:T], m, u8[:, 0, h:h + 1], 0.0, ALU.subtract, ALU.max)
                    last = v.tensor_scalar(decay[:, h, T:BLK], m[:, P:T], u8[:, 1, h:h + 1], 0.0,
                                           ALU.subtract, ALU.max)
                emptied(last, ("Mbc", i))
            conv_tile(6)
            conv_tile(7)
            v.memset(vx[:, :, :, MD:MD + 1], 1.0)
            for u in range(2):
                b = await_full(dve, ("mv", u, 1))
                emptied(v.tensor_copy(vx[:, 1, 2 * u:2 * u + 2, 0:MD], by_k(b, 2)), ("mv", u, 1))

            def score(h):
                b = await_full(dve, ("s", h))
                dve.wait_ge(dm_s, h + 1)
                dve.wait_ge(m_s, 1)
                if h >= 2:
                    await_copied(dve, ("num", h - 2, 1))
                ins = v.scalar_tensor_tensor(sdec[:, h % 2, :], b[:, 0:BLK], MD ** -0.5, decay[:, h, :],
                                             ALU.mult, ALU.mult)
                emptied(ins, ("s", h))

            vst = small[:, 84:96].rearrange("p (a n) -> p a n", a=2)
            score(0)
            score(1)
            vmv = spatial_stat
            for tt in range(NT):
                for u in range(2):
                    await_copied(dve, ("mz", u, tt))
                for u in range(2):
                    last = v.bn_stats(vst[:, u, :], zv[:, tt, NB * u:NB * u + NB])
                link(last)
                last = v.bn_aggr(vmv[:, tt, :], vst.rearrange("p a n -> p (a n)"))
                if tt == 0:
                    link(last)
            last.then_inc(var_ready, 1)
            dve.wait_ge(inv_ready, 1)
            link(v.reciprocal(spatial_var, spatial_var))
            dve.wait_ge(gsg_s, 32)
            for tt in range(NT):
                z = zv[:, tt, :]
                link(v.tensor_scalar(z, z, vmv[:, tt, 0:1], vmv[:, tt, 1:2], ALU.subtract, ALU.mult))
                link(v.tensor_tensor(z, z, gain_sg, ALU.mult))
                v.tensor_tensor(z, z, gain_sb, ALU.add).then_inc(vn_s, 1)
            score(2)
            score(3)
            stat = conv[:, 0, 0:48].rearrange("p (a n) -> p a n", a=8)
            mv = conv[:, 0, 48:64].rearrange("p (a n) -> p a n", a=8)
            nd, nv = conv[:, 0, 64:72], head_var
            dve.wait_ge(qk_s, 8)
            for n in range(8):
                await_copied(dve, ("num", n // 2, n % 2))
                last = v.bn_stats(stat[:, n, :], hm[:, n, 0:MD])
            link(last)
            for n in range(8):
                last = v.bn_aggr(mv[:, n, :], stat[:, n, :])
            link(last)
            dve.wait_ge(em_s, 1)
            dens = hm[:, :, MD:MD + 1].rearrange("p (h t) o -> p h (t o)", h=MH)
            nd3 = nd.rearrange("p (h t) -> p h t", h=MH)
            link(v.scalar_tensor_tensor(nd3, dens, -1.0, dens, ALU.mult, ALU.max))
            link(v.tensor_tensor(nd3, nd3, m8.rearrange("p t h -> p h t"), ALU.max))
            link(v.reciprocal(nd, nd))
            link(v.tensor_tensor(nv, mv[:, :, 1], nd, ALU.mult))
            v.tensor_tensor(nv, nv, nd, ALU.mult).then_inc(var_ready, 1)
            dve.wait_ge(inv_ready, 2)
            link(v.reciprocal(nv, nv))
            link(v.tensor_tensor(nv, nv, nd, ALU.mult))
            for n in range(8):
                last = v.tensor_scalar(hm[:, n, 0:MD], hm[:, n, 0:MD], mv[:, n, 0:1], nv[:, n:n + 1],
                                       ALU.subtract, ALU.mult)
            link(last)
            for tt in range(NT):
                dve.wait_ge(hg_s, tt + 1)
                h4 = hm.rearrange("p (h t) n -> p h t n", h=MH)[:, :, tt, 0:MD]
                last = v.tensor_tensor(hn[:, tt, :].rearrange("p (h n) -> p h n", h=MH), h4,
                                       sig_gm[:, tt, :].rearrange("p (h n) -> p h n", h=MH), ALU.mult)
            link(last)
            for tt in range(NT):
                for half in range(2):
                    b = await_full(dve, ("sv", tt, half))
                    for i in range(2):
                        s = 2 * half + i
                        part = zu[:, tt, SGC * s:SGC * s + SGC]
                        ins = v.scalar_tensor_tensor(part, b[:, SGC * i:SGC * i + SGC], cols[:, 80 + s:81 + s], part,
                                                     ALU.add, ALU.mult)
                    emptied(ins, ("sv", tt, half))
            for u in range(2):
                for tt in range(NT):
                    await_copied(dve, ("sv", tt, u))
                    await_copied(dve, ("mgs", u, tt))
                    sl = slice(NB * u, NB * u + NB)
                    link(v.tensor_tensor(zu[:, tt, sl], zu[:, tt, sl], zv[:, tt, sl], ALU.mult))
                    ins = v.tensor_tensor(hn[:, tt, sl], hn[:, tt, sl], zu[:, tt, sl], ALU.add)
                    if u == 1:
                        ins.then_inc(hn_ready, 1)
            transposed(4)
            for u in range(2):
                for tt in range(NT):
                    b = await_full(dve, ("mout", u, tt))
                    part = x[:, tt, NB * u:NB * u + NB]
                    emptied(v.tensor_tensor(part, part, b, ALU.add), ("mout", u, tt))
            dve.wait_ge(gf2_s, 16)
            norm(5, gain_f2)
            transposed(5)
            ffn(1)
            dve.wait_ge(gfin_s, 16)
            norm(6, gain0[:])

        @block.tensor
        def _(pe):
            t = nc.tensor

            def transposes(j):
                for tt in range(NT):
                    pe.wait_ge(hn_ready, NT * j + tt + 1)
                    for half in range(2):
                        b = open_bank(pe, ("T", j, tt, half))
                        for i in range(4):
                            c = 4 * half + i
                            last = t.transpose(b[:, P * i:P * i + P], hn[:, tt, P * c:P * c + P], ident[:])
                        filled(last, ("T", j, tt, half))

            def await_hT(j):
                for tt in range(NT):
                    for half in range(2):
                        await_copied(pe, ("T", j, tt, half))

            def landed_a(u):
                n = at_a[u]
                pe.wait_ge(wa_in[n % RING_A], 32 * (n // RING_A + 1))
                return by_k(slot_a(n))

            def landed_b(u, k=KD):
                n = at_b[u]
                pe.wait_ge(wb_in[n % RING_B], 32 * (n // RING_B + 1))
                return by_k(slot_b(n), k)

            def token_unit(names, w, src):
                for tt, name in enumerate(names):
                    b = open_bank(pe, name)
                    for k in range(KD):
                        last = t.matmul(b, src[:, k, P * tt:P * tt + P], w[:, k, :],
                                        start=(k == 0), stop=(k == KD - 1))
                    filled(last, name)

            def feature_unit(names, w):
                for i, name in enumerate(names):
                    b = open_bank(pe, name)
                    for f in range(2):
                        for k in range(KD):
                            c = P * (2 * i + f)
                            last = t.matmul(b[:, T * f:T * f + T], w[:, k, c:c + P], hT[:, k, :],
                                            start=(k == 0), stop=(k == KD - 1))
                    filled(last, name)

            def ada(j):
                w = landed_a(("ada", j))
                b = open_bank(pe, ("ada", j))
                for k in range(KD):
                    last = t.matmul(b, crep[:, k, :], w[:, k, :], start=(k == 0), stop=(k == KD - 1))
                filled(last, ("ada", j))

            pe.wait_ge(consts, 11)
            pe.wait_ge(c_rep, 1)
            for j in range(4):
                ada(j)
            transposes(0)
            await_hT(0)
            for u in range(4):
                feature_unit([("qk", u, 0), ("qk", u, 1)], landed_a(("qkv", u)))
            for u in range(2):
                token_unit([("v", u, 0), ("v", u, 1)], landed_a(("qkv", 4 + u)), hT)

            for u in range(4):
                for i in range(2):
                    await_copied(pe, ("qk", u, i))
            for u in range(2):
                for tt in range(NT):
                    await_copied(pe, ("v", u, tt))
            for h in range(HEADS + 2):
                if h < HEADS:
                    po, f = DH * (h % 2), h // 2
                    q, k = qkT[po:po + DH, f, :], qkT[po:po + DH, KD + f, :]
                    b = open_bank(pe, ("z", h))
                    t.matmul(b[:, 0:T], k[:, 0:P], q, start=True, stop=True)
                    last = t.matmul(b[:, T:BLK], k[:, P:T], q[:, P:T], start=False, stop=True,
                                    skip_group_check=True)
                    filled(last, ("z", h))
                if 1 <= h <= HEADS:
                    g = h - 1
                    b, s = bank(("z", g)), att_sp[:, g % 2, :]
                    pe.wait_ge(z_spm, g + 1)
                    t.matmul(b[:, 0:T], neg_ge[:], s[:, 0:T], start=False, stop=True, skip_group_check=True)
                    t.matmul(b[:, P:T], neg_ones[:], s[:, T:BLK], start=False, stop=True, skip_group_check=True)
                    last = t.matmul(b[:, T:BLK], neg_ge[:], s[:, T:BLK], start=False, stop=True,
                                    skip_group_check=True)
                    filled(last, ("z", g))
                if h >= 2:
                    g = h - 2
                    po = DH * (g % 2)
                    b = open_bank(pe, ("o", g // 2)) if g % 2 == 0 else bank(("o", g // 2))
                    pe.wait_ge(z_am, g + 1)
                    w = att_a[:, g % 2, :]
                    t.matmul(b[po:po + DH, 0:T], vtok[:, 0, DH * g:DH * g + DH], w[:, 0:T], start=True, stop=False)
                    last = t.matmul(b[po:po + DH, P:T], vtok[:, 1, DH * g:DH * g + DH], w[:, T:BLK],
                                    start=False, stop=True)
                    last.then_inc(z_o, 1)
                if h < HEADS and h % 2 == 1:
                    ada(4 + h // 2)
            for p in range(KD):
                await_copied(pe, ("o", p))
            for u in range(2):
                token_unit([("out", u, 0), ("out", u, 1)], landed_a(("out", u)), oT)
            transposes(1)
            await_hT(1)

            pe.wait_ge(rt_s, 64)
            b = open_bank(pe, ("router", 0))
            for tt in range(NT):
                for k in range(KD):
                    last = t.matmul(b[:, 64 * tt:64 * tt + 36], hT[:, k, P * tt:P * tt + P], wr[:, k, :],
                                    start=(k == 0), stop=(k == KD - 1))
            filled(last, ("router", 0))
            chosen = route[:, 560:560 + NT * EXPERTS].rearrange("p (a n) -> p a n", a=NT)
            b = open_bank(pe, ("router", 1))
            pe.wait_ge(r_sel, 1)
            t.matmul(b[:, 0:32], lt[:], chosen[:, 0, :], start=True, stop=True)
            t.matmul(b[:, 32:64], ones[:], chosen[:, 0, :], start=True, stop=False)
            t.matmul(b[:, 32:64], lt[:], chosen[:, 1, :], start=False, stop=True)
            t.matmul(b[:, 64:96], ones[:], chosen[:, 0, :], start=True, stop=False)
            last = t.matmul(b[:, 64:96], ones[:], chosen[:, 1, :], start=False, stop=True)
            filled(last, ("router", 1))
            for name in [("T", 1, tt, i) for tt in range(NT) for i in range(2)] + [("router", 0), ("router", 1)]:
                await_copied(pe, name)

            def expert_group(it, S, first, landed):
                pe.wait_ge(S.acc, it + 1)
                pe.wait_ge(S.sel, it + 1)
                for c in range(KD):
                    for tt in range(NT):
                        t.matmul(psum[:, c // 4, P * (c % 4):P * (c % 4) + P], hn[:, tt, P * c:P * c + P],
                                 m_sel[:, tt].rearrange("p e s -> p (e s)"), start=(tt == 0), stop=(tt == NT - 1))
                for tt in range(NT):
                    last = t.transpose(psum[:, 3, P * tt:P * tt + P],
                                       m_wsel[:, tt].rearrange("p e s -> p (e s)"), ident[:])
                last.then_inc(S.x_full, 1)
                pe.wait_ge(S.xa, it + 1)
                pe.wait_ge(S.xv, it + 1)
                for u in range(KD):
                    n = first + u
                    pe.wait_ge(landed[n % RING_A], it * 64 + 32 * (n // RING_A + 1))
                    w = slot_a(n).rearrange("p (w e n) -> p w e n", w=2, e=EG)
                    for i in range(2):
                        for e in range(EG):
                            last = t.matmul(psum[CAP * e:CAP * e + CAP, 4 + i, :], m_xT[:, u, CAP * e:CAP * e + CAP],
                                            w[:, i, e, :], start=(u == 0), stop=(u == KD - 1))
                    last.then_inc(S.used, 1)
                pe.wait_ge(S.h, it + 1)
                for f in range(KF_E):
                    last = t.transpose(psum[:, 2, P * f:P * f + P], m_h[:, P * f:P * f + P], ident[:])
                last.then_inc(S.hT_full, 1)
                pe.wait_ge(S.hT, it + 1)
                for f in range(KF_E):
                    n = first + KD + f
                    pe.wait_ge(landed[n % RING_A], it * 64 + 32 * (n // RING_A + 1))
                    w = slot_a(n).rearrange("p (e n) -> p e n", e=EG)
                    for half in range(2):
                        for e in range(EG):
                            last = t.matmul(psum[CAP * e:CAP * e + CAP, 6 + half, :], m_hT[:, f, CAP * e:CAP * e + CAP],
                                            w[:, e, NB * half:NB * half + NB], start=(f == 0), stop=(f == KF_E - 1))
                    last.then_inc(S.used, 1)
                pe.wait_ge(S.ya, it + 1)
                pe.wait_ge(S.yv, it + 1)
                for tt in range(NT):
                    for half in range(2):
                        last = t.matmul(psum[:, 2 * tt + half, :], m_wT[:, tt, :], m_y[:, NB * half:NB * half + NB],
                                        start=True, stop=True)
                last.then_inc(S.c_full, 1)

            with pe.Fori(0, NEG) as g:
                expert_group(g, main, NA, wa_in)
            pe.wait_ge(r_done, 1)
            longest = pe.value_load(maxcount[:], min_val=0, max_val=T)
            with pe.If(longest > CAP):
                pe.sem_inc(over.used, RING_A)
                with pe.Fori(0, ROUNDS - 1) as r:
                    with pe.Fori(0, NEG) as g:
                        expert_group(r * NEG + g, over, 0, over_in)
                pe.wait_ge(over.acc, (ROUNDS - 1) * NEG + 1)
            pe.end_ifs()
            pe.wait_ge(main.acc, NEG + 1)

            transposes(2)

            def ffn(n):
                for j in range(n_in):
                    w = landed_b(("in", n, j))
                    for i, kind in enumerate(("gate", "up")):
                        b = open_bank(pe, (kind, n, j))
                        for f in range(2):
                            for k in range(KD):
                                c = 256 * i + P * f
                                last = t.matmul(b[:, T * f:T * f + T], w[:, k, c:c + P], hT[:, k, :],
                                                start=(k == 0), stop=(k == KD - 1))
                        filled(last, (kind, n, j))
                banks = [open_bank(pe, ("down", n, i)) for i in range(4)]
                for j in range(n_out):
                    w = landed_b(("down", n, j), 4)
                    for i in range(min(4, NF - 4 * j)):
                        c = 4 * j + i
                        if c % 2 == 0:
                            await_copied(pe, ("up", n, c // 2))
                        for tt in range(NT):
                            for half in range(2):
                                last = t.matmul(banks[2 * tt + half], actT[:, c, P * tt:P * tt + P],
                                                w[:, i, NB * half:NB * half + NB], start=(c == 0), stop=(c == NF - 1))
                                if c == NF - 1:
                                    filled(last, ("down", n, 2 * tt + half))
                    if j < n_out - 1:
                        last.then_inc(down_used, 1)

            await_hT(2)
            ffn(0)
            pe.wait_ge(colrow_s, 48)
            b = open_bank(pe, ("cols",))
            filled(t.transpose(b[:, 0:84], rows84[:], ident[0:84, 0:84]), ("cols",))
            b = open_bank(pe, ("ws",))
            pe.wait_ge(ws_s, 16)
            for s in range(SG):
                last = t.transpose(b[:, P * s:P * s + P], wrows[:, s, :], ident[:])
            filled(last, ("ws",))
            transposes(3)
            await_hT(3)

            pe.wait_ge(if_s, 48)
            b = open_bank(pe, ("if",))
            for tt in range(NT):
                for k in range(KD):
                    last = t.matmul(b[:, 8 * tt:8 * tt + 8], hT[:, k, P * tt:P * tt + P], wif[:, k, :],
                                    start=(k == 0), stop=(k == KD - 1))
            filled(last, ("if",))
            lf = small[:, 120:128].rearrange("p (a n) -> p a n", a=NT)
            u8 = small[:, 128:136].rearrange("p (a n) -> p a n", a=NT)
            mT = sdec[0:MH, 0, 0:T]
            for u in range(4):
                kind, j = mix_units[u]
                feature_unit([("cq", u, 0), ("cq", u, 1)], landed_b(("mix", kind, j)))
                if u == 0:
                    b = open_bank(pe, ("B",))
                    pe.wait_ge(lf_s, 1)
                    t.matmul(b[:, 0:4], le[:], lf[:, 0, :], start=True, stop=True)
                    t.matmul(b[:, 4:8], ones[:], lf[:, 0, :], start=True, stop=False)
                    filled(t.matmul(b[:, 4:8], le[:], lf[:, 1, :], start=False, stop=True), ("B",))
                if u == 1:
                    b = open_bank(pe, ("uT",))
                    pe.wait_ge(u_s, 1)
                    t.transpose(b[0:MH, 0:P], u8[:, 0, :], ident[:])
                    filled(t.transpose(b[0:MH, P:T], u8[:, 1, :], ident[:]), ("uT",))
                if u == 2:
                    pe.wait_ge(m_s, 1)
                    for i in range(2):
                        b = open_bank(pe, ("Mbc", i))
                        for h in range(2):
                            last = t.matmul(b[:, T * h:T * h + T], pick[:, 2 * i + h, :], mT, start=True, stop=True)
                        filled(last, ("Mbc", i))
                    b = open_bank(pe, ("Mt",))
                    t.transpose(b[:, 0:MH], mT[:, 0:P], ident[0:MH, 0:MH])
                    filled(t.transpose(b[:, MH:2 * MH], mT[:, P:T], ident[0:MH, 0:MH]), ("Mt",))

            def token_mix(kind, j, name):
                token_unit([(name[0], name[1], tt) for tt in range(NT)], landed_b(("mix", kind, j)), hT)

            for u in range(2):
                token_mix("v", u, ("mv", u))
            for u in range(4):
                token_mix("z", (2, 3, 0, 1)[u], ("mz", u))
                h = u
                if u == 0:
                    pe.wait_ge(qk_s, 8)
                b = open_bank(pe, ("s", h))
                for i in range(2):
                    q, k = mqkT[:, 2 * h + i, :], mqkT[:, KD + 2 * h + i, :]
                    t.matmul(b[:, 0:T], k[:, 0:P], q, start=(i == 0), stop=(i == 1), skip_group_check=True)
                    last = t.matmul(b[:, T:BLK], k[:, P:T], q[:, P:T], start=False, stop=(i == 1),
                                    skip_group_check=True)
                filled(last, ("s", h))
            for u in range(2):
                token_mix("o", u, ("mo", u))
                if u == 0:
                    for i in range(2):
                        for tt in range(NT):
                            await_copied(pe, ("mv", i, tt))
                for h in (2 * u, 2 * u + 1):
                    await_copied(pe, ("s", h))
                    s = sdec[:, h % 2, :]
                    b = open_bank(pe, ("num", h, 0))
                    filled(t.matmul(b[:, 0:MD + 1], s[:, 0:P], vx[:, 0, h, :], start=True, stop=True), ("num", h, 0))
                    b = open_bank(pe, ("num", h, 1))
                    t.matmul(b[:, 0:MD + 1], s[:, P:T], vx[:, 0, h, :], start=True, stop=False)
                    filled(t.matmul(b[:, 0:MD + 1], s[:, T:BLK], vx[:, 1, h, :], start=False, stop=True), ("num", h, 1))
            for u in range(2):
                token_mix("gm", u, ("mgm", u))
            pe.wait_ge(ws_m, 1)
            for tt in range(NT):
                pe.wait_ge(vn_s, tt + 1)
                for half in range(2):
                    b = open_bank(pe, ("sv", tt, half))
                    for i in range(2):
                        s = 2 * half + i
                        last = t.matmul(b[:, SGC * i:SGC * i + SGC], wsT[:, s, :], zv[:, tt, SGC * s:SGC * s + SGC],
                                        start=True, stop=True)
                    filled(last, ("sv", tt, half))
            for u in range(2):
                token_mix("gs", u, ("mgs", u))
            transposes(4)
            await_hT(4)
            for u in range(2):
                token_unit([("mout", u, 0), ("mout", u, 1)], landed_b(("mout", u)), hT)
            transposes(5)
            await_hT(5)
            ffn(1)


_INS = ["x", "c", "ada_w", "ada_b", "norm_g", "final_g", "sb_w_in", "sb_w_out", "moe_w_grp", "moe_b_grp",
        "moe_w_exp", "moe_b_exp", "moe_w_gate", "moe_w_up", "moe_w_down", "ffn1_norm_g_2", "ffn1_w_in_2",
        "ffn1_w_out_2", "mix_norm_g_2", "w_mix_in_2", "mlstm_conv_w_2", "mlstm_conv_b_2", "mlstm_b_igate_2",
        "mlstm_b_fgate_2", "mlstm_head_norm_g_2", "sgu_norm_g_2", "sgu_norm_b_2", "sgu_w_s_2", "sgu_b_s_2",
        "w_mix_out_2", "ffn2_norm_g_2", "ffn2_w_in_2", "ffn2_w_out_2", "final_norm_g_2"]


def kernel(**inputs):
    import numpy as np
    import concourse.bacc as bacc
    from concourse.bass_utils import run_bass_kernel_spmd

    nc = bacc.Bacc("TRN2", target_bir_lowering=False, num_devices=1)
    arrays, args = {}, []
    for name in _INS:
        a = np.ascontiguousarray(inputs[name])
        arrays[f"in_{name}_dram"] = a
        args.append(nc.dram_tensor(f"in_{name}_dram", a.shape, FP32, kind="ExternalInput").ap())
    args.append(nc.dram_tensor("out_0_dram", (1, T, D), FP32, kind="ExternalOutput").ap())
    build_program(nc, *args)
    r = run_bass_kernel_spmd(nc, [arrays], core_ids=[0])
    return r.results[0]["out_0_dram"]
```
